# Optimizing a Trainium2 kernel written in Bass

```python
import math, functools
import jax, jax.numpy as jnp
from jax import lax
import numpy as np

D_MODEL = 1024
BATCH = 1
SEQ = 256
DEPTH = 2
DEC_BATCH = 8
DEC_SEQ = 8
PAST_LEN = 1024
PAGE_SIZE = 128

H_A = 6
H_B = 6
H_C = 4
N_HEADS_TOT = H_A + H_B + H_C
D_HEAD = D_MODEL // N_HEADS_TOT
D_MIX = N_HEADS_TOT * D_HEAD
D_C = D_HEAD // 2
H_IDX = 8
D_IDX = D_HEAD
TOPK_MAX = 256
DIL_CFG = ((128, 1), (512, 4), (2048, 16))
A_WIN = 2048
N_BUCKETS = 32
MAX_DIST = 128
D_FF = 4 * D_MODEL
Q_BLOCK = 128
DN_ALPHA = (2 * DEPTH) ** 0.25
DN_BETA = (8 * DEPTH) ** -0.25
LN_EPS = 1e-5
PROJ_SIZES = (H_A * D_HEAD, H_A * D_HEAD, H_A * D_HEAD,
              H_B * D_HEAD, H_B * D_HEAD, H_B * D_HEAD,
              H_IDX * D_IDX, D_IDX, H_IDX,
              H_C * 2 * D_C, H_C * 2 * D_C, H_C * 2 * D_C)
N_IN = sum(PROJ_SIZES)

kernel_name = 'hybrid_dilated_dsa_diff_decoder'

def rel_bucket(dist):
    n = jnp.maximum(dist, 0)
    exact = N_BUCKETS // 2
    nf = jnp.maximum(n, 1).astype(jnp.float32)
    large = exact + (jnp.log(nf / exact) / math.log(MAX_DIST / exact) * (N_BUCKETS - exact)).astype(jnp.int32)
    return jnp.where(n < exact, n, jnp.minimum(large, N_BUCKETS - 1))

def layer_norm(x, g, b):
    xf = x.astype(jnp.float32)
    mu = jnp.mean(xf, axis=-1, keepdims=True)
    var = jnp.mean(jnp.square(xf - mu), axis=-1, keepdims=True)
    y = (xf - mu) * lax.rsqrt(var + LN_EPS) * g.astype(jnp.float32) + b.astype(jnp.float32)
    return y.astype(x.dtype)

def adaln(c, w, b):
    m = jax.nn.silu(c) @ w + b
    sh, sc, g = jnp.split(m, 3, axis=-1)
    return sh[:, None], sc[:, None], g[:, None]

def split_heads(z):
    nb, t = z.shape[:2]
    parts, start = [], 0
    for size in PROJ_SIZES:
        parts.append(z[..., start:start + size])
        start += size
    qa, ka, va, qb, kb, vb, qi, ki, wi, qc, kc, vc = parts
    hd = lambda a, h: a.reshape(nb, t, h, -1)
    return (hd(qa, H_A), hd(ka, H_A), hd(va, H_A), hd(qb, H_B), hd(kb, H_B), hd(vb, H_B),
            hd(qi, H_IDX), ki, wi,
            qc.reshape(nb, t, H_C, 2, D_C), kc.reshape(nb, t, H_C, 2, D_C), vc.reshape(nb, t, H_C, 2 * D_C))

def dilated_attend(q, k_all, v_all, q_idx, rel_bias):
    qf = q.astype(jnp.float32) * D_HEAD ** -0.5
    outs, lses = [], []
    for win, dil in DIL_CFG:
        steps = jnp.arange(win // dil + 1) * dil
        kidx = q_idx[:, None] - steps[None, :]
        valid = kidx >= 0
        kidx = jnp.maximum(kidx, 0)
        kg = k_all[:, kidx].astype(jnp.float32)
        vg = v_all[:, kidx].astype(jnp.float32)
        bias = rel_bias[rel_bucket(steps)][:, :H_A].astype(jnp.float32).T
        s = jnp.einsum('bthd,btjhd->bhtj', qf, kg) + bias[None, :, None, :]
        s = jnp.where(valid[None, None], s, -jnp.inf)
        lse = jax.nn.logsumexp(s, axis=-1, keepdims=True)
        outs.append(jnp.einsum('bhtj,btjhd->bthd', jnp.exp(s - lse), vg))
        lses.append(lse[..., 0])
    mix = jax.nn.softmax(jnp.stack(lses), axis=0)
    o = jnp.einsum('cbht,cbthd->bthd', mix, jnp.stack(outs))
    return o.astype(q.dtype)

def dsa_attend(q, qi, wi, q_pos, ki_all, gather_kv, topk, rel_bias):
    L = ki_all.shape[1]
    dots = jnp.einsum('bthe,bse->bths', qi.astype(jnp.float32), ki_all.astype(jnp.float32)) * D_IDX ** -0.5
    score = jnp.einsum('bth,bths->bts', wi.astype(jnp.float32) * H_IDX ** -0.5, jax.nn.relu(dots))
    score = jnp.where(jnp.arange(L)[None, None, :] <= q_pos[None, :, None], score, -jnp.inf)
    _, sel = lax.top_k(score, topk)
    kg, vg = gather_kv(sel)
    dist = q_pos[None, :, None] - sel
    bias = rel_bias[rel_bucket(dist)][..., H_A:H_A + H_B].astype(jnp.float32)
    s = jnp.einsum('bthd,btkhd->bthk', q.astype(jnp.float32) * D_HEAD ** -0.5, kg.astype(jnp.float32))
    s = s + jnp.swapaxes(bias, 2, 3)
    s = jnp.where((dist >= 0)[:, :, None, :], s, -jnp.inf)
    p = jax.nn.softmax(s, axis=-1)
    o = jnp.einsum('bthk,btkhd->bthd', p, vg.astype(jnp.float32))
    return o.astype(q.dtype)

def diff_attend(q, k_all, v_all, q_pos, lam, lam_init, subln_g, rel_bias):
    L = k_all.shape[1]
    dist = q_pos[:, None] - jnp.arange(L)[None, :]
    bias = jnp.transpose(rel_bias[rel_bucket(dist)][..., H_A + H_B:].astype(jnp.float32), (2, 0, 1))
    s = jnp.einsum('bthmd,bshmd->bhmts', q.astype(jnp.float32) * D_C ** -0.5, k_all.astype(jnp.float32))
    s = jnp.where(dist >= 0, s + bias[None, :, None], -jnp.inf)
    p = jax.nn.softmax(s, axis=-1)
    lf = lam.astype(jnp.float32)
    lam_full = jnp.exp(jnp.sum(lf[0] * lf[1])) - jnp.exp(jnp.sum(lf[2] * lf[3])) + lam_init
    a = p[:, :, 0] - lam_full * p[:, :, 1]
    o = jnp.einsum('bhts,bshd->bthd', a, v_all.astype(jnp.float32))
    o = o * lax.rsqrt(jnp.mean(jnp.square(o), axis=-1, keepdims=True) + 1e-5)
    o = o * subln_g.astype(jnp.float32) * (1.0 - lam_init)
    return o.astype(q.dtype)

def prompt_mixer(heads, lam_l, subln_g_l, lam_init, rel_bias):
    qa, ka, va, qb, kb, vb, qi, ki, wi, qc, kc, vc = heads
    nb, s_len = qa.shape[:2]
    topk = min(TOPK_MAX, s_len // 4)
    bidx = jnp.arange(nb)[:, None, None]
    gather_kv = lambda sel: (kb[bidx, sel], vb[bidx, sel])

    def block(bi):
        t0 = bi * Q_BLOCK
        q_pos = t0 + jnp.arange(Q_BLOCK)
        blk = lambda a: lax.dynamic_slice_in_dim(a, t0, Q_BLOCK, axis=1)
        oa = dilated_attend(blk(qa), ka, va, q_pos, rel_bias)
        ob = dsa_attend(blk(qb), blk(qi), blk(wi), q_pos, ki, gather_kv, topk, rel_bias)
        oc = diff_attend(blk(qc), kc, vc, q_pos, lam_l, lam_init, subln_g_l, rel_bias)
        return jnp.concatenate([oa.reshape(nb, Q_BLOCK, -1), ob.reshape(nb, Q_BLOCK, -1),
                                oc.reshape(nb, Q_BLOCK, -1)], axis=-1)

    o = lax.map(block, jnp.arange(s_len // Q_BLOCK))
    o = jnp.moveaxis(o, 0, 1).reshape(nb, s_len, D_MIX)
    keep = min(A_WIN, s_len)
    state = (ka[:, s_len - keep:], va[:, s_len - keep:], kb, vb, ki, kc, vc)
    return o, state

def sample_mixer(heads, l, cache_a_k, cache_a_v, cache_b_k, cache_b_v, cache_b_ik, cache_c_k, cache_c_v,
                 page_table, lam_l, subln_g_l, lam_init, rel_bias):
    qa, ka, va, qb, kb, vb, qi, ki, wi, qc, kc, vc = heads
    nb, t = qa.shape[:2]
    past = page_table.shape[1] * PAGE_SIZE
    q_pos = past + jnp.arange(t)
    bidx = jnp.arange(nb)[:, None, None]

    def paged_rows(pool):
        rows = pool[l, page_table]
        return rows.reshape((nb, past) + rows.shape[3:])

    wbuf = cache_a_k.shape[2]
    ka_all = jnp.concatenate([cache_a_k[l], ka], axis=1)
    va_all = jnp.concatenate([cache_a_v[l], va], axis=1)
    oa = dilated_attend(qa, ka_all, va_all, wbuf + jnp.arange(t), rel_bias)

    ki_all = jnp.concatenate([paged_rows(cache_b_ik), ki], axis=1)

    def gather_kv(sel):
        old = jnp.minimum(sel, past - 1)
        phys = page_table[bidx, old // PAGE_SIZE]
        off = old % PAGE_SIZE
        new = jnp.clip(sel - past, 0, t - 1)
        is_past = (sel < past)[..., None, None]
        kg = jnp.where(is_past, cache_b_k[l, phys, off], kb[bidx, new])
        vg = jnp.where(is_past, cache_b_v[l, phys, off], vb[bidx, new])
        return kg, vg

    ob = dsa_attend(qb, qi, wi, q_pos, ki_all, gather_kv, min(TOPK_MAX, (past + t) // 4), rel_bias)

    kc_all = jnp.concatenate([paged_rows(cache_c_k), kc], axis=1)
    vc_all = jnp.concatenate([paged_rows(cache_c_v), vc], axis=1)
    oc = diff_attend(qc, kc_all, vc_all, q_pos, lam_l, lam_init, subln_g_l, rel_bias)

    o = jnp.concatenate([oa.reshape(nb, t, -1), ob.reshape(nb, t, -1), oc.reshape(nb, t, -1)], axis=-1)
    n_all = ka_all.shape[1]
    keep = min(A_WIN, n_all)
    state = (ka_all[:, n_all - keep:], va_all[:, n_all - keep:], kb, vb, ki, kc, vc)
    return o, state

def run_layer(x, c, mixer, w_ada_mix_l, b_ada_mix_l, w_in_l, w_o_l, ln1_g_l, ln1_b_l,
              w_ada_mlp_l, b_ada_mlp_l, w_up_l, w_down_l, ln2_g_l, ln2_b_l):
    sh, sc, g = adaln(c, w_ada_mix_l, b_ada_mix_l)
    h = x * (1 + sc) + sh
    o, state = mixer(split_heads(h @ w_in_l))
    x = layer_norm(DN_ALPHA * x + (1 + g) * (o @ w_o_l), ln1_g_l, ln1_b_l)
    sh, sc, g = adaln(c, w_ada_mlp_l, b_ada_mlp_l)
    h = x * (1 + sc) + sh
    f = jnp.square(jax.nn.relu(h @ w_up_l)) @ w_down_l
    x = layer_norm(DN_ALPHA * x + (1 + g) * f, ln2_g_l, ln2_b_l)
    return x, state

def setup_inputs(seed: int = 0) -> dict:
    key = jax.random.key(seed)
    ks = jax.random.split(key, 32)
    n_pages = PAST_LEN // PAGE_SIZE
    n_used = DEC_BATCH * n_pages
    n_phys = n_used + max(1, n_used // 4)
    wa = min(A_WIN, PAST_LEN)
    nrm = lambda k, shape, s=1.0: jax.random.normal(k, shape, jnp.float32) * s
    page_table = jax.random.permutation(ks[9], n_phys)[:n_used].reshape(DEC_BATCH, n_pages).astype(jnp.int32)
    return {
        'x_prompt': nrm(ks[0], (BATCH, SEQ, D_MODEL)),
        'x_sample': nrm(ks[1], (DEC_BATCH, DEC_SEQ, D_MODEL)),
        'cache_a_k': nrm(ks[2], (DEPTH, DEC_BATCH, wa, H_A, D_HEAD)),
        'cache_a_v': nrm(ks[3], (DEPTH, DEC_BATCH, wa, H_A, D_HEAD)),
        'cache_b_k': nrm(ks[4], (DEPTH, n_phys, PAGE_SIZE, H_B, D_HEAD)),
        'cache_b_v': nrm(ks[5], (DEPTH, n_phys, PAGE_SIZE, H_B, D_HEAD)),
        'cache_b_ik': nrm(ks[6], (DEPTH, n_phys, PAGE_SIZE, D_IDX)),
        'cache_c_k': nrm(ks[7], (DEPTH, n_phys, PAGE_SIZE, H_C, 2, D_C)),
        'cache_c_v': nrm(ks[8], (DEPTH, n_phys, PAGE_SIZE, H_C, 2 * D_C)),
        'page_table': page_table,
        'c_prompt': nrm(ks[10], (BATCH, D_MODEL)),
        'c_sample': nrm(ks[11], (DEC_BATCH, D_MODEL)),
        'rel_bias': nrm(ks[12], (N_BUCKETS, N_HEADS_TOT), 0.5),
        'w_ada_mix': nrm(ks[13], (DEPTH, D_MODEL, 3 * D_MODEL), 0.1 * D_MODEL ** -0.5),
        'b_ada_mix': nrm(ks[14], (DEPTH, 3 * D_MODEL), 0.01),
        'w_in': nrm(ks[15], (DEPTH, D_MODEL, N_IN), D_MODEL ** -0.5),
        'lam': nrm(ks[16], (DEPTH, 4, D_C), 0.1),
        'subln_g': 1.0 + nrm(ks[17], (DEPTH, 2 * D_C), 0.01),
        'w_o': nrm(ks[18], (DEPTH, D_MIX, D_MODEL), DN_BETA * D_MIX ** -0.5),
        'ln1_g': 1.0 + nrm(ks[19], (DEPTH, D_MODEL), 0.01),
        'ln1_b': nrm(ks[20], (DEPTH, D_MODEL), 0.01),
        'w_ada_mlp': nrm(ks[21], (DEPTH, D_MODEL, 3 * D_MODEL), 0.1 * D_MODEL ** -0.5),
        'b_ada_mlp': nrm(ks[22], (DEPTH, 3 * D_MODEL), 0.01),
        'w_up': nrm(ks[23], (DEPTH, D_MODEL, D_FF), D_MODEL ** -0.5),
        'w_down': nrm(ks[24], (DEPTH, D_FF, D_MODEL), DN_BETA * D_FF ** -0.5),
        'ln2_g': 1.0 + nrm(ks[25], (DEPTH, D_MODEL), 0.01),
        'ln2_b': nrm(ks[26], (DEPTH, D_MODEL), 0.01),
    }

def reference(x_prompt, x_sample, cache_a_k, cache_a_v, cache_b_k, cache_b_v, cache_b_ik, cache_c_k, cache_c_v,
              page_table, c_prompt, c_sample, rel_bias, w_ada_mix, b_ada_mix, w_in, lam, subln_g, w_o,
              ln1_g, ln1_b, w_ada_mlp, b_ada_mlp, w_up, w_down, ln2_g, ln2_b):
    xp, xs = x_prompt, x_sample
    p_states, s_states = [], []
    for l in range(DEPTH):
        lam_init = 0.8 - 0.6 * math.exp(-0.3 * l)
        lw = (w_ada_mix[l], b_ada_mix[l], w_in[l], w_o[l], ln1_g[l], ln1_b[l],
              w_ada_mlp[l], b_ada_mlp[l], w_up[l], w_down[l], ln2_g[l], ln2_b[l])
        pm = functools.partial(prompt_mixer, lam_l=lam[l], subln_g_l=subln_g[l], lam_init=lam_init,
                               rel_bias=rel_bias)
        sm = functools.partial(sample_mixer, l=l, cache_a_k=cache_a_k, cache_a_v=cache_a_v,
                               cache_b_k=cache_b_k, cache_b_v=cache_b_v, cache_b_ik=cache_b_ik,
                               cache_c_k=cache_c_k, cache_c_v=cache_c_v, page_table=page_table,
                               lam_l=lam[l], subln_g_l=subln_g[l], lam_init=lam_init, rel_bias=rel_bias)
        xp, sp = run_layer(xp, c_prompt, pm, *lw)
        xs, ss = run_layer(xs, c_sample, sm, *lw)
        p_states.append(sp)
        s_states.append(ss)
    stk = lambda states, i: jnp.stack([st[i] for st in states])
    p_a_k, p_a_v, p_b_k, p_b_v = stk(p_states, 0), stk(p_states, 1), stk(p_states, 2), stk(p_states, 3)
    p_b_ik, p_c_k, p_c_v = stk(p_states, 4), stk(p_states, 5), stk(p_states, 6)
    s_a_k, s_a_v, s_b_k, s_b_v = stk(s_states, 0), stk(s_states, 1), stk(s_states, 2), stk(s_states, 3)
    s_b_ik, s_c_k, s_c_v = stk(s_states, 4), stk(s_states, 5), stk(s_states, 6)
    return (xp, xs, p_a_k, p_a_v, p_b_k, p_b_v, p_b_ik, p_c_k, p_c_v,
            s_a_k, s_a_v, s_b_k, s_b_v, s_b_ik, s_c_k, s_c_v)


_drawn_inputs = setup_inputs


def setup_inputs(seed=0):
    import zlib

    import numpy as np

    out = dict(_drawn_inputs(seed))
    spreads = {}
    factors = {'b_ada_mix': 3.554,
     'lam': 5.257,
     'subln_g': 8.0,
     'ln1_g': 3.764,
     'ln1_b': 3.546,
     'b_ada_mlp': 4.778,
     'ln2_g': 3.676,
     'ln2_b': 3.635}
    for name, (base, spread) in spreads.items():
        noise = np.random.default_rng([zlib.crc32(name.encode()), seed]).standard_normal(out[name].shape)
        drawn = base * np.exp(spread * noise) if base else spread * noise
        out[name] = __import__('jax').numpy.asarray(drawn.astype(out[name].dtype))
    for name, factor in factors.items():
        out[name] = (out[name] * factor).astype(out[name].dtype)
    return out
```

```python
import math
from contextlib import ExitStack

import numpy as np

import concourse.bass as bass
from concourse import mybir

F32 = mybir.dt.float32
BF16 = mybir.dt.bfloat16
I32 = mybir.dt.int32
ALU = mybir.AluOpType
ACT = mybir.ActivationFunctionType
AX_X = mybir.AxisListType.X
ds = bass.ds

P = 128
D = 1024
KD = D // P
DEPTH = 2
TP = 256
NB = 8
NT = 8
TS = NB * NT
T = TP + TS
PAST = 1024
L = PAST + NT
PAGE = 128
NPG = PAST // PAGE
N_PHYS = 80
HA = HB = 6
HC = 4
HI = 8
H = HA + HB + HC
DH = 64
DC = 32
FF = 4096
NCOND = 1 + NB
TOPK_P = min(256, TP // 4)
TOPK_S = min(256, L // 4)
ALPHA = (2 * DEPTH) ** 0.25
EPS = 1e-5
FAR = -1e30
TAKEN = -3e38
LAM_INIT = [0.8 - 0.6 * math.exp(-0.3 * l) for l in range(DEPTH)]

QI, QA, QB, QC, KA, KB, KC, KI, WI = 0, 4, 7, 10, 12, 15, 18, 20, 21
NZ = 22
VA, VB, VC = 0, 384, 768

ADA_T, V_T, FEAT_T, WO_T, UP_T, DOWN_T = 48, 8, 20, 8, 32, 32
RING = 4
V_AT = ADA_T
FEAT_AT = V_AT + V_T
WO_AT = FEAT_AT + FEAT_T
UP_AT = WO_AT + WO_T
DOWN_AT = UP_AT + UP_T
TILES = DOWN_AT + DOWN_T

DIST0 = L - 1
NDIST = DIST0 + P
NEAR0 = DIST0 - TP + 1
NEAR_W = NDIST - NEAR0 + 1

RA, RC = HA * NT, 2 * HC * NT
AB_W = 768
C_W = 512
AC_UNITS, UNITS = 2 * NB, 3 * NB
ITEMS = 16
AB_LOADS = 4 * 2 * 16 + 4 * NPG * 16

P_ADA, P_LN, P_SUB, P_NLAM, P_COEF = 0, 48, 80, 81, 82
NPAR = 83


class Signal:

    def __init__(self, sem, per, spare=0):
        self.sem, self.per, self.spare = sem, per, spare

    def done(self, l, n):
        return l * self.per + (n + 1 + self.spare)

    def free(self, l, n):
        return l * self.per + (n + 1)


class Unit:

    def __init__(self, n, kind, b, s, v, nth):
        self.n, self.kind, self.b, self.s, self.v, self.nth = n, kind, b, s, v, nth
        self.rows = RC if kind == "C" else RA
        self.width = HC * DH if kind == "C" else HA * DH
        self.v0 = {"A": VA, "B": VB, "C": VC}[kind]


def unit_ac(i, r):
    return Unit(4 * i + r, "AC"[r % 2], 2 * i + r // 2, r % 2, r // 2 % 2, i + r // 4)


def unit_b(i, r):
    return Unit(AC_UNITS + 2 * i + r, "B", 2 * i + r, r % 2, r % 2, i + r // 2)


def item(n):
    qt, g = n // 8, n % 8
    return qt, g, (P if qt == 0 else TP), (2 if g < 6 else 4)


def repeat(ap, n):
    return bass.AP(ap.tensor, ap.offset, [*[list(x) for x in ap.ap], [0, n]])


def program(nc, a, out):
    ctx = ExitStack()
    with ctx:
        def sb(name, shape, dt=F32):
            return ctx.enter_context(nc.sbuf_tensor(name, shape, dt))

        def sem(name):
            return ctx.enter_context(nc.semaphore(name))

        xT = sb("xT", [P, KD, T])
        hT = sb("hT", [P, KD, T])
        oT = hT
        zT = sb("zT", [P, NZ, T])
        vp = sb("vp", [P, 2, D])
        vs = sb("vs", [TS, D])
        vnew = sb("vnew", [NT, 2, D])
        pbias = sb("pbias", [P, H, TP])
        sbiasA = sb("sbiasA", [RA, L])
        sbiasB = sb("sbiasB", [RA, L])
        sbiasC = sb("sbiasC", [RC, L])
        ring = sb("ring", [P, RING, KD, P])
        wki = sb("wki", [P, KD, P + HI])
        big = sb("big", [P, 2 * NPG * AB_W])
        ab = big[:, :].rearrange("p (s j w) -> p s j w", s=2, j=NPG)
        uT = big[:, 0:FF // P * T].rearrange("p (m t) -> p m t", t=T)
        cbuf = sb("cbuf", [P, NPG * C_W])
        cs = cbuf[:, :].rearrange("p (j w) -> p j w", j=NPG)
        ik = cbuf[:, 0:2 * NPG * P].rearrange("p (s j w) -> p s j w", s=2, j=NPG)
        adarow = cbuf[0:NCOND, 0:3 * D]
        onehot = big[0:34, 0:NDIST]
        distb = big[0:H, 2048:2048 + NDIST]
        qab = sb("qab", [P, 2, 3 * RA])
        qc = sb("qc", [P, 2 * RC])
        qi = sb("qi", [P, 2, HI * NT])
        wall = sb("wall", [HI * NT, NB, TS])
        S = sb("S", [P, 2, L])
        PT = sb("PT", [P, 2, 9, 64])
        osb = sb("osb", [64, 2, 384])
        work = sb("work", [TS, L])
        sel = sb("sel", [TS, L], BF16)
        psc = sb("psc", [P, 384])
        psel = sb("psel", [P, 384], BF16)
        adaT = sb("adaT", [P, 2, 24, NCOND])
        par_all = sb("par_all", [P, DEPTH, NPAR])
        par = sb("par", [P, NPAR])
        sq = sb("sq", [P, 2, T])
        rstd = sb("rstd", [P, T])
        tmp = sq[:, 0, :]
        ident = sb("ident", [P, P])
        ident16 = sb("ident16", [P, P], BF16)
        onesd = sb("onesd", [P, P])
        oneshd = sb("oneshd", [P, P])
        zscale = sb("zscale", [P, NZ])
        cT = sb("cT", [P, KD, NCOND])
        sgm = sb("sgm", [P, KD, NCOND])
        relb = sb("relb", [34, H])
        rep = sb("rep", [HI, HI * NT])
        tmask = sb("tmask", [HI * NT, TS])
        selB = sb("selB", [TS, NB, RA], BF16)
        sumC = sb("sumC", [RC, 32])
        ismap1 = sb("ismap1", [P, 2])
        zero16 = sb("zero16", [P, 512], BF16)
        wcur = sb("wcur", [HI * NT, 2, TS])
        kin = sb("kin", [P, 2, NT])
        selcur = sb("selcur", [TS, 2, RA], BF16)
        smask = sb("smask", [TS, NT])
        lamb = S[:, 0, 0:DEPTH * 4 * DC].rearrange("p (l a d) -> p l a d", l=DEPTH, a=4)
        lp = S[:, 1, 0:DEPTH * 2 * DC].rearrange("p (e d) -> p e d", d=DC)
        ls = sb("ls", [P, DEPTH * 2])
        cmask = sb("cmask", [P, TP])
        ptab = sb("ptab", [1, NB * NPG], I32)
        wiq = sb("wiq", [P, 2, HI])
        m8 = sb("m8", [P, 2, 8])
        mx = sb("mx", [P, 2, 4])
        nmx = sb("nmx", [P, 2, 4])
        sm = sb("sm", [P, 2, 4])
        rs = sb("rs", [P, 2, 4])
        PTf = PT[:, :, :, :].rearrange("p s j r -> p s (j r)")
        psel_at = [TP, 0]
        dist_s = nc.dram_tensor("dist_sample", [H, NT, NDIST], F32, kind="Internal").ap()
        dist_p = nc.dram_tensor("dist_prompt", [P, H, NEAR_W], F32, kind="Internal").ap()

        psf = ctx.enter_context(nc.psum_tensor("psf", [P, 8 * 512], F32))
        bank = [psf[:, 512 * i:512 * i + 512] for i in range(8)]

        passed = sem("passed")
        ld_const = sem("ld_const")
        ld_w = [sem(f"ld_w{s}") for s in range(RING)]
        ld_wki = sem("ld_wki")
        ld_ik = [sem(f"ld_ik{s}") for s in range(2)]
        ld_ab = [sem(f"ld_ab{s}") for s in range(2)]
        ld_c = sem("ld_c")
        ld_vnew = [sem(f"ld_vnew{s}") for s in range(2)]
        ld_dist = sem("ld_dist")
        st_dist = sem("st_dist")
        st_a = [sem(f"st_a{s}") for s in range(2)]
        st_state = sem("st_state")
        st_y = sem("st_y")
        zeroed = sem("zeroed")
        dist_ps = sem("dist_ps")
        dist_sb = sem("dist_sb")
        sig_exp = sem("sig_exp")
        silu_done = sem("silu_done")
        lam_sum = sem("lam_sum")
        lam_exp = sem("lam_exp")
        tile_used = Signal(sem("tile_used"), TILES, RING)
        ada_row = Signal(sem("ada_row"), 12, 2)
        ada_tp = Signal(sem("ada_tp"), 2)
        ada_set = Signal(sem("ada_set"), 2)
        h_set = Signal(sem("h_set"), 2)
        v_set = Signal(sem("v_set"), 6)
        z_ps = Signal(sem("z_ps"), 2)
        z_set = Signal(sem("z_set"), NZ, 2)
        wi_ps = Signal(sem("wi_ps"), 1)
        wi_set = Signal(sem("wi_set"), 1)
        pd_ps = Signal(sem("pd_ps"), 2 * HI)
        pd_relu = Signal(sem("pd_relu"), 2 * HI, 2)
        pd_acc = Signal(sem("pd_acc"), 2 * HI, 2)
        psel_set = Signal(sem("psel_set"), 1)
        qi_set = Signal(sem("qi_set"), NB)
        sd_ps = Signal(sem("sd_ps"), NB)
        sd_relu = Signal(sem("sd_relu"), NB, 2)
        sc_ps = Signal(sem("sc_ps"), NB, 2)
        sc_sum = Signal(sem("sc_sum"), 1)
        sc_copied = Signal(sem("sc_copied"), 1)
        sel_set = Signal(sem("sel_set"), 1)
        q_set = Signal(sem("q_set"), UNITS)
        u_s = Signal(sem("u_s"), UNITS, 2)
        u_logit = Signal(sem("u_logit"), UNITS, 2)
        u_exp = Signal(sem("u_exp"), UNITS)
        u_tp = Signal(sem("u_tp"), UNITS, 2)
        u_tset = Signal(sem("u_tset"), UNITS, 1)
        u_o = Signal(sem("u_o"), UNITS, 2)
        u_oset = Signal(sem("u_oset"), UNITS, 1)
        u_ot = Signal(sem("u_ot"), UNITS)
        u_out = Signal(sem("u_out"), UNITS, 2)
        i_s = Signal(sem("i_s"), ITEMS)
        i_logit = Signal(sem("i_logit"), ITEMS, 2)
        i_exp = Signal(sem("i_exp"), ITEMS)
        i_p = Signal(sem("i_p"), ITEMS)
        i_tp = Signal(sem("i_tp"), ITEMS, 2)
        i_tset = Signal(sem("i_tset"), ITEMS, 2)
        i_o = Signal(sem("i_o"), ITEMS, 2)
        i_out = Signal(sem("i_out"), ITEMS, 2)
        gn_sq = Signal(sem("gn_sq"), 1)
        gn_ps = Signal(sem("gn_ps"), 1)
        gn_var = Signal(sem("gn_var"), 1)
        gn_std = Signal(sem("gn_std"), 1)
        gn_set = Signal(sem("gn_set"), 1)
        wo_set = Signal(sem("wo_set"), KD, 2)
        dn_set = Signal(sem("dn_set"), KD, 2)
        ln_mean = Signal(sem("ln_mean"), 2)
        ln_xc = Signal(sem("ln_xc"), 2 * KD)
        ln_sq = Signal(sem("ln_sq"), 2 * KD)
        ln_mm = Signal(sem("ln_mm"), 2 * KD, 2)
        ln_var = Signal(sem("ln_var"), 2)
        ln_std = Signal(sem("ln_std"), 2)
        ln_n = Signal(sem("ln_n"), 2 * KD)
        ln_x = Signal(sem("ln_x"), 2 * KD, 1)
        up_relu = Signal(sem("up_relu"), FF // P, 2)
        up_set = Signal(sem("up_set"), FF // P, 2)

        def last_keys(u):
            return psf[0:NT, 1536 * u.s + 1024 + 64:1536 * u.s + 1024 + 64 + u.rows]

        def outputs_at(u):
            return 1536 * (1 - u.s) + 1024 + 128

        block = ctx.enter_context(nc.Block())

        consts = [(xT[:], a["x"]), (ident[:], a["ident"]), (ident16[:], a["ident16"]), (onesd[:], a["onesd"]),
                  (oneshd[:], a["oneshd"]), (zscale[:], a["zscale"]), (cT[:], a["cond"]),
                  (relb[0:32, :], a["rel_bias"]), (relb[32:34, :], a["relrows"]), (onehot, a["onehot"]),
                  (rep[:], a["rep"]), (tmask[:], a["tmask"]), (selB[:], a["selB"]), (sumC[:], a["sumC"]),
                  (ismap1[:], a["ismap1"]), (cmask[:], a["cmask"]), (smask[:], a["smask"]),
                  (ptab[:], a["page_table"]), (par_all[:, :, 0:P_NLAM], a["params"])]
        N_CONST = 16 * (len(consts) + 1)
        N_DIST = 16 * (2 + 2 * HC + 1)

        @block.sync
        def _(sp):
            for dst, src in consts:
                sp.dma_start(dst, src).then_inc(ld_const, 16)
            sp.dma_start(S[:, 0, 0:DEPTH * 4 * DC], a["lam"].to_broadcast([P, DEPTH * 4 * DC])
                         ).then_inc(ld_const, 16)
            def tiles(l, at, n):
                sp.sem_inc(passed, 1)
                with sp.Fori(0, n // RING) as i:
                    for s in range(RING):
                        sp.wait_ge(tile_used.sem, tile_used.free(l, at + RING * i + s))
                        sp.dma_start(ring[:, s].rearrange("p k m -> p (k m)"),
                                     a["tiles"][ds(l * TILES + at + RING * i + s, 1)].rearrange("o p w -> (o p) w")
                                     ).then_inc(ld_w[s], 16)

            def page(l, b, j):
                return sp.value_load(ptab[0:1, ds(b * NPG + j, 1)], min_val=0, max_val=N_PHYS - 1) + l * N_PHYS

            def load_a(l, b, s):
                for j in range(2):
                    sp.dma_start(ab[:, s, 4 * j:4 * j + 4, :].rearrange("p j w -> p (j w)"),
                                 a["cache_a"][ds(l * NB + b, 1), :, 4 * j * AB_W:4 * (j + 1) * AB_W]
                                 .rearrange("o p w -> (o p) w")).then_inc(ld_ab[s], 16)

            def load_pages(l, b, pool, dst, signal):
                sp.sem_inc(passed, 1)
                for j in range(NPG):
                    sp.dma_start(dst[:, j, :], pool[ds(page(l, b, j), 1)].rearrange("o p w -> (o p) w")
                                 ).then_inc(signal, 16)

            def load_ik(l, b, s):
                sp.sem_inc(passed, 1)
                for j in range(NPG):
                    pg = page(l, b, j)
                    for half in range(2):
                        sp.dma_start(ik[64 * half:64 * half + 64, s, j, :],
                                     a["pool_ik"][ds(pg, 1)].rearrange("o p w -> (o p) w")).then_inc(ld_ik[s], 16)

            def load_vnew(l, b, s):
                sp.dma_start(vnew[:, s, :], out["vs"][ds(l, 1), ds(b * NT, NT), :].rearrange("o t w -> (o t) w")
                             ).then_inc(ld_vnew[s], 16)

            with sp.Fori(0, DEPTH) as l:
                tiles(l, 0, ADA_T)
                sp.wait_ge(st_dist, 32)
                for b in range(2):
                    load_a(l, b, b)
                tiles(l, V_AT, V_T)
                sp.wait_ge(ada_tp.sem, ada_tp.done(l, 1))
                for b in range(2):
                    load_ik(l, b, b)
                sp.dma_start(wki[:], a["wki"][ds(l, 1)].rearrange("o p k m -> (o p) k m")).then_inc(ld_wki, 16)
                tiles(l, FEAT_AT, FEAT_T)
                sp.wait_ge(v_set.sem, v_set.done(l, 5))
                sp.dma_start(out["vs"][ds(l, 1)].rearrange("o p t -> (o p) t"), vs[:]).then_inc(st_state, 16)
                sp.dma_start(out["vp"][ds(l, 1)].rearrange("o p k t -> (o p) k t"), vp[:]).then_inc(st_state, 16)
                sp.wait_ge(st_state, 48 * l + 32)
                for b in range(2):
                    load_vnew(l, b, b)
                sp.wait_ge(z_set.sem, z_set.done(l, NZ - 1))
                sp.dma_start(out["z"][ds(l, 1)].rearrange("o p k t -> (o p) k t"), zT[:, KA:KI + 1, :]
                             ).then_inc(st_state, 16)
                with sp.Fori(0, 3) as i:
                    for s in range(2):
                        sp.wait_ge(sd_ps.sem, sd_ps.done(l, 2 * i + s))
                        load_ik(l, 2 * i + 2 + s, s)
                sp.wait_ge(sd_ps.sem, sd_ps.done(l, NB - 1))
                load_pages(l, 0, a["pool_c"], cs, ld_c)
                tiles(l, WO_AT, RING)
                with sp.Fori(0, 3) as i:
                    for s in range(2):
                        sp.wait_ge(u_o.sem, u_o.done(l, 4 * i + 2 * s))
                        sp.wait_ge(st_a[s], 64 * l + 16 * i + 16)
                        load_a(l, 2 * i + 2 + s, s)
                        sp.wait_ge(u_o.sem, u_o.done(l, 4 * i + 2 * s + 1))
                        load_pages(l, 2 * i + 1 + s, a["pool_c"], cs, ld_c)
                        load_vnew(l, 2 * i + 2 + s, s)
                sp.wait_ge(u_o.sem, u_o.done(l, AC_UNITS - 3))
                load_pages(l, NB - 1, a["pool_c"], cs, ld_c)
                for s in range(2):
                    sp.wait_ge(u_o.sem, u_o.done(l, AC_UNITS - 4 + 2 * s))
                    sp.wait_ge(st_a[s], 64 * l + 64)
                    load_pages(l, s, a["pool_b"], ab[:, s], ld_ab[s])
                    sp.wait_ge(u_o.sem, u_o.done(l, AC_UNITS - 3 + 2 * s))
                    load_vnew(l, s, s)
                with sp.Fori(0, 3) as i:
                    for s in range(2):
                        sp.wait_ge(u_o.sem, u_o.done(l, AC_UNITS + 2 * i + s))
                        load_pages(l, 2 * i + 2 + s, a["pool_b"], ab[:, s], ld_ab[s])
                        load_vnew(l, 2 * i + 2 + s, s)
                tiles(l, WO_AT + RING, WO_T - RING)
                tiles(l, UP_AT, UP_T)
                sp.wait_ge(st_state, 48 * l + 48)
                tiles(l, DOWN_AT, DOWN_T)
            sp.wait_ge(ln_x.sem, ln_x.done(DEPTH - 1, 2 * KD - 1))
            sp.dma_start(out["y"], xT[:]).then_inc(st_y, 16)
            sp.wait_ge(st_y, 16)
            sp.wait_ge(st_a[0], 64 * DEPTH)
            sp.wait_ge(st_a[1], 64 * DEPTH)
            sp.wait_ge(st_state, 48 * DEPTH)

        @block.gpsimd
        def _(pool):
            for t in (qab, qc, qi, wall, zero16):
                ins = pool.memset(t[:], 0.0)
            pool.drain()
            pool.sem_inc(zeroed, 1)
            with pool.Fori(0, DEPTH) as l:
                pool.wait_ge(z_set.sem, z_set.done(l, NZ - 1))
                pool.wait_ge(wi_set.sem, wi_set.done(l, 0))
                pool.sem_inc(passed, 1)
                with pool.Fori(0, NB // 2) as i:
                    for s in range(2):
                        pool.wait_ge(sc_ps.sem, sc_ps.free(l, 2 * i + s))
                        for half in range(2):
                            q = slice(64 * half, 64 * half + 64)
                            pool.tensor_copy(qi[q, s, :].rearrange("p (c e t) -> p c e t", e=2, t=NT)[:, :, half, :],
                                             zT[q, QI:QI + 4, ds(TP + NT * (2 * i + s), NT)])
                            pool.drain()
                        pool.tensor_copy(kin[:, s, :], zT[:, KI, ds(TP + NT * (2 * i + s), NT)])
                        pool.drain()
                        pool.tensor_copy(wcur[:, s, :], wall[:, ds(2 * i + s, 1), :].rearrange("p o t -> p (o t)"))
                        pool.drain()
                        pool.sem_inc(qi_set.sem, 1)

                def queries(u):
                    pool.wait_ge(u_s.sem, u_s.free(l, u.n))
                    if u.kind == "C":
                        for g in range(4):
                            q = slice(32 * g, 32 * g + 32)
                            first = qc[q, NT * g:NT * g + NT]
                            pool.tensor_copy(bass.AP(first.tensor, first.offset, [list(first.ap[0]), [96, 2], [1, NT]]),
                                             zT[q, QC:QC + 2, ds(TP + NT * u.b, NT)])
                            pool.drain()
                    else:
                        c0, s = (QA, 0) if u.kind == "A" else (QB, u.s)
                        for half in range(2):
                            q = slice(64 * half, 64 * half + 64)
                            first = qab[q, s, NT * half:NT * half + NT]
                            pool.tensor_copy(bass.AP(first.tensor, first.offset, [list(first.ap[0]), [64, 3], [1, NT]]),
                                             zT[q, c0:c0 + 3, ds(TP + NT * u.b, NT)])
                            pool.drain()
                        if u.kind == "B":
                            pool.tensor_copy(selcur[:, s, :], selB[:, ds(u.b, 1), :].rearrange("p o r -> p (o r)"))
                    pool.drain()
                    pool.sem_inc(q_set.sem, 1)

                with pool.Fori(0, NB // 2) as i:
                    for r in range(4):
                        queries(unit_ac(i, r))
                with pool.Fori(0, NB // 2) as i:
                    for r in range(2):
                        queries(unit_b(i, r))

        @block.scalar
        def _(act):
            for signal in (ada_row, z_set, pd_relu, sd_relu, i_tset, up_relu, ln_x):
                act.sem_inc(signal.sem, signal.spare)
            act.wait_ge(ld_const, N_CONST)
            act.activation(sgm[:], cT[:], ACT.Exp, scale=-1.0).then_inc(sig_exp, 1)
            act.wait_ge(lam_sum, 1)
            act.activation(ls[:], ls[:], ACT.Exp).then_inc(lam_exp, 1)
            act.wait_ge(dist_sb, 3)
            act.dma_start(dist_s.rearrange("h t u -> h t u"), bass.AP(distb.tensor, distb.offset,
                          [list(distb.ap[0]), [0, NT], [1, NDIST]])).then_inc(st_dist, 16)
            near = distb[:, NEAR0:NDIST]
            act.dma_start(dist_p[:, :, 0:NDIST - NEAR0].rearrange("p h u -> h p u"), bass.AP(near.tensor, near.offset,
                          [list(near.ap[0]), [0, P], [1, NDIST - NEAR0]])).then_inc(st_dist, 16)
            act.wait_ge(st_dist, 32)
            row = NT * NDIST
            for dst, h0 in ((sbiasA, 0), (sbiasB, HA)):
                act.dma_start(dst[:], bass.AP(dist_s.tensor, h0 * row + NT - 1, [[row, HA], [NDIST - 1, NT], [1, L]])
                              ).then_inc(ld_dist, 16)
            for r in range(2 * HC):
                act.dma_start(sbiasC[r * NT:r * NT + NT, :],
                              bass.AP(dist_s.tensor, (HA + HB + r // 2) * row + NT - 1, [[NDIST - 1, NT], [1, L]])
                              ).then_inc(ld_dist, 16)
            act.dma_start(pbias[:], bass.AP(dist_p.tensor, DIST0 - P - NEAR0,
                                            [[H * NEAR_W - 1, P], [NEAR_W, H], [1, TP]])).then_inc(ld_dist, 16)
            with act.Fori(0, DEPTH) as l:
                for half in range(2):
                    if half:
                        act.wait_ge(ada_tp.sem, ada_tp.done(l, 0))
                    with act.Fori(0, 3) as i:
                        for k in range(2):
                            act.wait_ge(tile_used.sem, tile_used.done(l, 24 * half + 8 * i + 4 * k + 3))
                            act.activation(adarow[:, ds(1024 * i + 512 * k, 512)], bank[6 + k][0:NCOND, :],
                                           ACT.Copy).then_inc(ada_row.sem, 1)
                with act.Fori(0, FEAT_T // 4) as i:
                    for k in range(4):
                        act.wait_ge(tile_used.sem, tile_used.done(l, FEAT_AT + 4 * i + k))
                        act.activation(zT[:, ds(4 * i + k, 1), :].rearrange("p o t -> p (o t)"), bank[6 + k % 2][:, 0:T],
                                       ACT.Copy, scale=zscale[:, ds(4 * i + k, 1)]).then_inc(z_set.sem, 1)
                act.wait_ge(z_ps.sem, z_ps.done(l, 0))
                act.activation(zT[:, KI, :], bank[6][:, 0:T], ACT.Copy).then_inc(z_set.sem, 1)
                act.wait_ge(z_ps.sem, z_ps.done(l, 1))
                act.activation(zT[0:HI, WI, :], bank[7][0:HI, 0:T], ACT.Copy, scale=float(HI) ** -0.5
                               ).then_inc(z_set.sem, 1)
                for n in range(2 * HI):
                    w = P if n < HI else TP
                    act.wait_ge(pd_ps.sem, pd_ps.done(l, n))
                    act.wait_ge(pd_acc.sem, pd_acc.free(l, n))
                    act.activation(S[:, n % 2, 0:w], bank[1 + n % 2][:, 0:w], ACT.Relu).then_inc(pd_relu.sem, 1)
                act.wait_ge(pd_acc.sem, pd_acc.done(l, 2 * HI - 1))
                with act.Fori(0, NB // 2) as i:
                    for s in range(2):
                        act.wait_ge(sd_ps.sem, sd_ps.done(l, 2 * i + s))
                        act.wait_ge(sc_ps.sem, sc_ps.free(l, 2 * i + s))
                        act.activation(S[0:64, s, 0:PAST], psf[0:64, 1024 * s:1024 * s + PAST], ACT.Relu)
                        act.activation(S[0:64, s, PAST:L], bank[4][64 * s:64 * s + 64, 0:NT], ACT.Relu
                                       ).then_inc(sd_relu.sem, 1)

                def exp_unit(u):
                    act.wait_ge(u_logit.sem, u_logit.done(l, u.n))
                    v = S[0:u.rows, u.s, :]
                    act.activation(v, v, ACT.Exp, bias=nmx[0:u.rows, u.s, 0:1], accum_out=sm[0:u.rows, u.s, 0:1]
                                   ).then_inc(u_exp.sem, 1)

                with act.Fori(0, NB // 2) as i:
                    for r in range(4):
                        u = unit_ac(i, r)
                        exp_unit(u)
                        if u.kind == "A":
                            act.wait_ge(ld_ab[u.v], AB_LOADS * l + 32 * u.nth + 32)
                            act.dma_start(out["cache_a"][ds(l * NB + u.b, 1)].rearrange("o p w -> (o p) w"),
                                          ab[:, u.v].rearrange("p j w -> p (j w)")).then_inc(st_a[u.v], 16)
                with act.Fori(0, NB // 2) as i:
                    for r in range(2):
                        exp_unit(unit_b(i, r))

                def exp_item(n):
                    qt, g, w, maps = item(n)
                    act.wait_ge(i_logit.sem, i_logit.done(l, n))
                    for m in range(maps):
                        v = S[:, n % 2, w * m:w * m + w]
                        ins = act.activation(v, v, ACT.Exp, bias=nmx[:, n % 2, m:m + 1],
                                             accum_out=sm[:, n % 2, m:m + 1])
                    ins.then_inc(i_exp.sem, 1)

                exp_item(0)
                for n in range(ITEMS):
                    if n + 1 < ITEMS:
                        exp_item(n + 1)
                    qt, g, w, maps = item(n)
                    act.wait_ge(i_tp.sem, i_tp.done(l, n))
                    act.wait_ge(i_o.sem, i_o.free(l, n))
                    act.activation(PTf[:, n % 2, 0:2 * w], bank[4 + n % 2][:, 0:2 * w], ACT.Copy
                                   ).then_inc(i_tset.sem, 1)
                act.wait_ge(gn_var.sem, gn_var.done(l, 0))
                act.activation(sq[:], sq[:], ACT.Sqrt).then_inc(gn_std.sem, 1)

                def norm(j):
                    for k in range(KD):
                        act.wait_ge(ln_xc.sem, ln_xc.done(l, KD * j + k))
                        act.wait_ge(ln_mm.sem, ln_mm.free(l, KD * j + k))
                        act.activation(sq[:, k % 2, :], xT[:, k, :], ACT.Square).then_inc(ln_sq.sem, 1)
                    act.wait_ge(ln_var.sem, ln_var.done(l, j))
                    act.activation(rstd[:], rstd[:], ACT.Sqrt).then_inc(ln_std.sem, 1)
                    for k in range(KD):
                        act.wait_ge(ln_n.sem, ln_n.done(l, KD * j + k))
                        g = P_LN + 2 * KD * j + k
                        act.activation(xT[:, k, :], xT[:, k, :], ACT.Identity, scale=par[:, g:g + 1],
                                       bias=par[:, g + KD:g + KD + 1]).then_inc(ln_x.sem, 1)

                norm(0)
                with act.Fori(0, UP_T // 4) as i:
                    for k in range(4):
                        act.wait_ge(tile_used.sem, tile_used.done(l, UP_AT + 4 * i + k))
                        act.wait_ge(up_set.sem, up_set.free(l, 4 * i + k))
                        act.activation(sq[:, k % 2, :], bank[6 + k % 2][:, 0:T], ACT.Relu).then_inc(up_relu.sem, 1)
                norm(1)

        @block.tensor
        def _(pe):
            for signal in (tile_used, u_s, u_tp, u_o, i_tp, i_o, ln_mm, sc_ps):
                pe.sem_inc(signal.sem, signal.spare)
            pe.wait_ge(ld_const, N_CONST)
            for c, (u0, u1) in enumerate(((0, 512), (512, 1024), (1024, NDIST))):
                pe.matmul(bank[c][0:H, 0:u1 - u0], relb[:], big[0:34, u0:u1], start=True, stop=True).then_inc(dist_ps, 1)
            pe.wait_ge(silu_done, 1)
            pe.wait_ge(zeroed, 1)

            def logits(l, u):
                pe.wait_ge(q_set.sem, q_set.done(l, u.n))
                pe.wait_ge(u_logit.sem, u_logit.free(l, u.n))
                if not (isinstance(u.n, int) and u.n < 3):
                    pe.wait_ge(u_out.sem, u_out.done(l, u.n - 3))
                if u.kind == "C":
                    kv, chunks, k0 = cs, 2, KC
                    pe.wait_ge(ld_c, NB * NPG * 16 * l + NPG * 16 * u.b + NPG * 16)
                else:
                    kv, chunks, k0 = ab[:, u.v], 3, (KA if u.kind == "A" else KB)
                    if u.kind == "A":
                        pe.wait_ge(ld_ab[u.v], AB_LOADS * l + 32 * u.nth + 32)
                    else:
                        pe.wait_ge(ld_ab[u.v], AB_LOADS * l + 128 + NPG * 16 * u.nth + NPG * 16)
                for q in range(3):
                    w = 512 if q < 2 else NT
                    dst = psf[0:u.rows, 1536 * u.s + 512 * q:1536 * u.s + 512 * q + w]
                    for c in range(chunks):
                        if u.kind == "C":
                            lhs = qc[:, RC * c:RC * c + RC]
                        else:
                            lhs = qab[:, 0 if u.kind == "A" else u.s, RA * c:RA * c + RA]
                        if q < 2:
                            rhs = kv[:, 4 * q:4 * q + 4, P * c:P * c + P]
                        else:
                            rhs = zT[:, k0 + c, ds(TP + NT * u.b, NT)]
                        ins = pe.matmul(dst, lhs, rhs, start=c == 0, stop=c == chunks - 1 and u.kind != "B")
                    if u.kind == "B":
                        ins = pe.matmul(dst, selcur[:, u.s, :], sel[:, 512 * q:512 * q + w], start=False, stop=True)
                ins.then_inc(u_s.sem, 1)

            def turn(l, u):
                pe.wait_ge(u_exp.sem, u_exp.done(l, u.n))
                pe.wait_ge(u_tset.sem, u_tset.free(l, u.n))
                pe.sem_inc(passed, 1)
                r = u.rows
                for j in range(NPG):
                    pe.transpose(bank[6][:, r * j:r * j + r], S[0:r, u.s, P * j:P * j + P], ident[0:r, 0:r])
                pe.transpose(last_keys(u), S[0:r, u.s, PAST:L], ident[0:r, 0:r]).then_inc(u_tp.sem, 1)

            def values(l, u):
                pe.wait_ge(u_tset.sem, u_tset.done(l, u.n))
                pe.wait_ge(u_oset.sem, u_oset.free(l, u.n))
                pe.wait_ge(ld_vnew[u.v], 2 * 64 * l + (64 if u.kind == "B" else 0) + 16 * u.nth + 16)
                dst = bank[7][0:u.rows, 0:u.width]
                for j in range(NPG):
                    rhs = cs[:, j, 2 * P:C_W] if u.kind == "C" else ab[:, u.v, j, 3 * P:AB_W]
                    pe.matmul(dst, PT[:, u.s, j, 0:u.rows], rhs, start=j == 0, stop=False)
                pe.matmul(dst, PT[0:NT, u.s, NPG, 0:u.rows], vnew[:, u.v, u.v0:u.v0 + u.width], start=False, stop=True
                          ).then_inc(u_o.sem, 1)

            def turn_out(l, u):
                pe.wait_ge(u_oset.sem, u_oset.done(l, u.n))
                pe.wait_ge(u_out.sem, u_out.free(l, u.n))
                pe.sem_inc(passed, 1)
                c0 = outputs_at(u)
                if u.kind == "C":
                    for c in range(2):
                        ins = pe.matmul(psf[:, c0 + 32 * c:c0 + 32 * c + 32], osb[:, u.s, P * c:P * c + P], sumC[:],
                                        start=True, stop=True)
                else:
                    for c in range(3):
                        ins = pe.transpose(psf[:, c0 + RA * c:c0 + RA * c + RA], osb[0:RA, u.s, P * c:P * c + P],
                                           ident[0:RA, 0:RA])
                ins.then_inc(u_ot.sem, 1)

            def step(l, unit, i, r, prev=True, following=True):
                turn(l, unit(i, r))
                if following:
                    logits(l, unit(i, r + 1))
                pe.wait_ge(u_tset.sem, u_tset.done(l, unit(i, r).n))
                if prev:
                    turn_out(l, unit(i, r - 1))
                values(l, unit(i, r))

            def ring_wait(l, s, at, i=0):
                pe.wait_ge(ld_w[s], l * (16 * TILES // RING) + 16 * (at // RING) + 16 * i + 16)

            def wide(s, kk):
                return ring[:, s].rearrange("p (e b) m -> p e (b m)", e=2)[:, kk, :]

            def chunks(l, at, n, rhs, freed):
                pe.sem_inc(passed, 1)
                with pe.Fori(0, n // RING) as i:
                    for s in range(RING):
                        pe.wait_ge(freed.sem, freed.free(l, RING * i + s))
                        ring_wait(l, s, at, i)
                        for k in range(KD):
                            ins = pe.matmul(bank[6 + s % 2][:, 0:T], ring[:, s, k, :], rhs[:, k, :],
                                            start=k == 0, stop=k == KD - 1)
                        ins.then_inc(tile_used.sem, 1)

            def norm_sums(l, j, summed):
                for k in range(KD):
                    pe.wait_ge(summed.sem, summed.done(l, k))
                    ins = pe.matmul(bank[0][:, 0:T], onesd[:], xT[:, k, :], start=k == 0, stop=k == KD - 1)
                ins.then_inc(ln_mean.sem, 1)
                for k in range(KD):
                    pe.wait_ge(ln_sq.sem, ln_sq.done(l, KD * j + k))
                    pe.matmul(bank[1][:, 0:T], onesd[:], sq[:, k % 2, :], start=k == 0, stop=k == KD - 1
                              ).then_inc(ln_mm.sem, 1)

            with pe.Fori(0, DEPTH) as l:
                pe.wait_ge(dn_set.sem, dn_set.free(l, 1))
                pe.sem_inc(passed, 1)
                for half in range(2):
                    with pe.Fori(0, 3) as i:
                        for k in range(2):
                            pe.wait_ge(ada_row.sem, ada_row.free(l, 6 * half + 2 * i + k))
                            for s in range(RING):
                                ring_wait(l, s, 24 * half + RING * k, 2 * i)
                                for kk in range(2):
                                    ins = pe.matmul(bank[6 + k][0:NCOND, :], cT[:, 2 * s + kk, :], wide(s, kk),
                                                    start=s + kk == 0, stop=s == RING - 1 and kk == 1)
                                ins.then_inc(tile_used.sem, 1)
                    pe.wait_ge(ada_row.sem, ada_row.done(l, 6 * half + 5))
                    pe.sem_inc(passed, 1)
                    for c in range(24):
                        ins = pe.transpose(bank[2 + half][:, NCOND * c:NCOND * c + NCOND], adarow[:, P * c:P * c + P],
                                           ident[0:NCOND, 0:NCOND])
                    ins.then_inc(ada_tp.sem, 1)
                pe.wait_ge(h_set.sem, h_set.done(l, 0))
                pe.wait_ge(ada_set.sem, ada_set.done(l, 1))
                for g in range(2):
                    for s in range(RING):
                        ring_wait(l, s, V_AT + RING * g)
                        for kk in range(2):
                            for tt in range(3):
                                m = P if tt < 2 else TS
                                ins = pe.matmul(bank[3 * g + tt][0:m, :], hT[:, 2 * s + kk, P * tt:P * tt + m],
                                                wide(s, kk), start=s + kk == 0, stop=s == RING - 1 and kk == 1)
                        ins.then_inc(tile_used.sem, 1)
                chunks(l, FEAT_AT, FEAT_T, hT, z_set)
                pe.wait_ge(ld_wki, 16 * l + 16)
                for c, m in ((KI, P), (WI, HI)):
                    pe.wait_ge(z_set.sem, z_set.free(l, c))
                    for k in range(KD):
                        ins = pe.matmul(bank[6 + c % 2][0:m, 0:T], wki[:, k, P * (c - KI):P * (c - KI) + m], hT[:, k, :],
                                        start=k == 0, stop=k == KD - 1)
                    ins.then_inc(z_ps.sem, 1)
                pe.wait_ge(z_set.sem, z_set.done(l, WI))
                pe.wait_ge(v_set.sem, v_set.done(l, 5))
                pe.sem_inc(passed, 1)
                for qt in range(2):
                    pe.transpose(bank[0][:, HI * qt:HI * qt + HI], zT[0:HI, WI, P * qt:P * qt + P], ident[0:HI, 0:HI])
                pe.matmul(bank[0][0:64, 64:128], rep[:], zT[0:HI, WI, TP:T], start=True, stop=True
                          ).then_inc(wi_ps.sem, 1)
                for n in range(2 * HI):
                    qt, h = n // HI, n % HI
                    w = P if qt == 0 else TP
                    q = slice(64 * (h % 2), 64 * (h % 2) + 64)
                    pe.wait_ge(pd_relu.sem, pd_relu.free(l, n))
                    pe.matmul(bank[1 + n % 2][:, 0:w], zT[q, QI + h // 2, P * qt:P * qt + P], zT[q, KI, 0:w],
                              start=True, stop=True).then_inc(pd_ps.sem, 1)
                pe.wait_ge(pd_relu.sem, pd_relu.done(l, 2 * HI - 1))
                pe.wait_ge(wi_set.sem, wi_set.done(l, 0))
                spans = ((0, 512), (1, 512), (2, NT))
                for q, w in spans:
                    pe.matmul(bank[5 + q][0:TS, 0:w], zero16[:, 0:TS], zero16[:, 0:w], start=True, stop=False)
                with pe.Fori(0, NB // 2) as i:
                    for s in range(2):
                        pe.wait_ge(qi_set.sem, qi_set.done(l, 2 * i + s))
                        pe.wait_ge(ld_ik[s], NB * NPG * 16 * l + 2 * NPG * 16 * i + 2 * NPG * 16)
                        pe.wait_ge(sd_relu.sem, sd_relu.free(l, 2 * i + s))
                        for q in range(2):
                            pe.matmul(bank[2 * s + q][0:64, :], qi[:, s, :], ik[:, s, 4 * q:4 * q + 4, :],
                                      start=True, stop=True)
                        pe.matmul(bank[4][64 * s:64 * s + 64, 0:NT], qi[:, s, :],
                                  kin[:, s, :], start=True, stop=True).then_inc(sd_ps.sem, 1)
                    for s in range(2):
                        pe.wait_ge(sd_relu.sem, sd_relu.done(l, 2 * i + s))
                        pe.sem_inc(passed, 1)
                        for q, w in spans:
                            ins = pe.matmul(bank[5 + q][0:TS, 0:w], wcur[:, s, :], S[0:64, s, 512 * q:512 * q + w],
                                            start=False, stop=False)
                        ins.then_inc(sc_ps.sem, 1)
                for q, w in spans:
                    ins = pe.matmul(bank[5 + q][0:TS, 0:w], zero16[:, 0:TS], zero16[:, 0:w], start=False, stop=True)
                ins.then_inc(sc_sum.sem, 1)
                pe.wait_ge(sc_copied.sem, sc_copied.done(l, 0))
                logits(l, unit_ac(0, 0))
                step(l, unit_ac, 0, 0, prev=False)
                with pe.Fori(0, 3) as i:
                    for r in range(1, 5):
                        step(l, unit_ac, i, r)
                for r in range(1, 4):
                    step(l, unit_ac, 3, r, following=r < 3)
                turn_out(l, unit_ac(3, 3))
                pe.wait_ge(sel_set.sem, sel_set.done(l, 0))
                pe.wait_ge(u_out.sem, u_out.done(l, AC_UNITS - 1))
                logits(l, unit_b(0, 0))
                step(l, unit_b, 0, 0, prev=False)
                with pe.Fori(0, 3) as i:
                    for r in range(1, 3):
                        step(l, unit_b, i, r)
                step(l, unit_b, 3, 1, following=False)
                turn_out(l, unit_b(3, 1))

                def item_logits(n):
                    qt, g, w, maps = item(n)
                    s = n % 2
                    pe.wait_ge(i_logit.sem, i_logit.free(l, n))
                    for m in range(maps):
                        if m == 2:
                            pe.drain()
                        at = 1024 * s + 512 * (m % 2) + w * (m // 2)
                        dst = psf[:, at:at + w]
                        if g < 6:
                            q, cq, ck = slice(64 * m, 64 * m + 64), QA + g, KA + g
                        else:
                            q, cq, ck = slice(32 * m, 32 * m + 32), QC + g - 6, KC + g - 6
                        topk = 3 <= g < 6
                        ins = pe.matmul(dst, zT[q, cq, P * qt:P * qt + P], zT[q, ck, 0:w], start=True, stop=not topk)
                        if topk:
                            ins = pe.matmul(dst, ident16[:], psel[:, psel_at[qt]:psel_at[qt] + w], start=False, stop=True)
                    ins.then_inc(i_s.sem, 1)

                pe.wait_ge(u_out.sem, u_out.done(l, UNITS - 1))
                pe.wait_ge(psel_set.sem, psel_set.done(l, 0))
                item_logits(0)
                for n in range(ITEMS):
                    if n + 1 < ITEMS:
                        item_logits(n + 1)
                    qt, g, w, maps = item(n)
                    s = n % 2
                    pe.wait_ge(i_p.sem, i_p.done(l, n))
                    pe.wait_ge(i_tset.sem, i_tset.free(l, n))
                    for kt in range(w // P):
                        for e in range(2):
                            m0 = w * (e if g < 6 else 2 * e) + P * kt
                            ins = pe.transpose(bank[4 + s][:, 2 * P * kt + P * e:2 * P * kt + P * e + P],
                                               S[:, s, m0:m0 + P], ident[:])
                    ins.then_inc(i_tp.sem, 1)
                    pe.wait_ge(i_tset.sem, i_tset.done(l, n))
                    pe.wait_ge(i_out.sem, i_out.free(l, n))
                    for kt in range(w // P):
                        ins = pe.matmul(bank[6 + s][:, 0:2 * P], vp[:, kt, P * g:P * g + P],
                                        PTf[:, s, 2 * P * kt:2 * P * kt + 2 * P], start=kt == 0, stop=kt == w // P - 1)
                    ins.then_inc(i_o.sem, 1)
                pe.wait_ge(gn_sq.sem, gn_sq.done(l, 0))
                for c in range(2):
                    ins = pe.matmul(bank[c][:, 0:T], oneshd[:], sq[:, c, :], start=True, stop=True)
                ins.then_inc(gn_ps.sem, 1)
                pe.wait_ge(gn_set.sem, gn_set.done(l, 0))
                chunks(l, WO_AT, WO_T, oT, wo_set)
                norm_sums(l, 0, wo_set)
                pe.wait_ge(h_set.sem, h_set.done(l, 1))
                chunks(l, UP_AT, UP_T, hT, up_relu)
                pe.wait_ge(up_set.sem, up_set.done(l, FF // P - 1))
                pe.sem_inc(passed, 1)
                with pe.Fori(0, KD // 2) as i:
                    for m in range(2):
                        pe.wait_ge(dn_set.sem, dn_set.free(l, 2 * i + m))
                        for s in range(RING):
                            ring_wait(l, s, DOWN_AT + RING * m, 2 * i)
                            for k in range(KD):
                                ins = pe.matmul(bank[6 + m][:, 0:T], ring[:, s, k, :], uT[:, KD * s + k, :],
                                                start=s + k == 0, stop=s == RING - 1 and k == KD - 1)
                            ins.then_inc(tile_used.sem, 1)
                norm_sums(l, 1, dn_set)

        @block.vector
        def _(dve):
            for signal in (pd_acc, u_logit, u_tset, u_oset, u_out, i_logit, i_out, wo_set, dn_set, up_set):
                dve.sem_inc(signal.sem, signal.spare)
            dve.wait_ge(ld_const, N_CONST)
            dve.tensor_tensor(lp.rearrange("p (l e) d -> p l e d", e=2), lamb[:, :, 0::2, :], lamb[:, :, 1::2, :],
                              ALU.mult)
            dve.drain()
            dve.tensor_reduce(ls[:], lp, AX_X, ALU.add).then_inc(lam_sum, 1)
            for c, (u0, u1) in enumerate(((0, 512), (512, 1024), (1024, NDIST))):
                dve.wait_ge(dist_ps, c + 1)
                dve.tensor_copy(distb[:, u0:u1], bank[c][0:H, 0:u1 - u0]).then_inc(dist_sb, 1)
            dve.wait_ge(sig_exp, 1)
            dve.tensor_scalar(sgm[:], sgm[:], 1.0, None, ALU.add)
            dve.drain()
            dve.reciprocal(sgm[:], sgm[:])
            dve.drain()
            dve.tensor_tensor(cT[:], cT[:], sgm[:], ALU.mult).then_inc(silu_done, 1)
            dve.wait_ge(lam_exp, 1)
            for l in range(DEPTH):
                nlam = par_all[:, l, P_NLAM:P_NLAM + 1]
                dve.tensor_tensor(nlam, ls[:, 2 * l + 1:2 * l + 2], ls[:, 2 * l:2 * l + 1], ALU.subtract)
                dve.drain()
                dve.tensor_scalar(nlam, nlam, -LAM_INIT[l], None, ALU.add)
                sub = par_all[:, l, P_SUB:P_SUB + 1]
                dve.tensor_scalar(sub, sub, 1.0 - LAM_INIT[l], None, ALU.mult)
                dve.drain()
                dve.scalar_tensor_tensor(par_all[:, l, P_COEF:P_COEF + 1], nlam, ismap1[:, 0:1], ismap1[:, 1:2],
                                         ALU.mult, ALU.add)
            dve.drain()
            dve.wait_ge(zeroed, 1)
            tokens = "p k (b t) -> p k b t"

            def modulation(l, j):
                dve.wait_ge(ada_tp.sem, ada_tp.done(l, j))
                b0 = P_ADA + 24 * j
                dve.tensor_tensor(adaT[:, j], bank[2 + j][:, 0:24 * NCOND].rearrange("p (c n) -> p c n", n=NCOND),
                                  repeat(par[:, b0:b0 + 24], NCOND), ALU.add)
                dve.drain()
                dve.tensor_scalar(adaT[:, j, KD:24, :], adaT[:, j, KD:24, :], 1.0, None, ALU.add
                                  ).then_inc(ada_set.sem, 1)
                dve.drain()

            def modulate(j):
                for k in range(KD):
                    dve.tensor_scalar(hT[:, k, 0:TP], xT[:, k, 0:TP], adaT[:, j, KD + k, 0:1], adaT[:, j, k, 0:1],
                                      ALU.mult, ALU.add)
                hs = hT[:, :, TP:T].rearrange(tokens, t=NT)
                dve.tensor_tensor(hs, xT[:, :, TP:T].rearrange(tokens, t=NT), repeat(adaT[:, j, KD:2 * KD, 1:NCOND], NT),
                                  ALU.mult)
                dve.drain()
                dve.tensor_tensor(hs, hs, repeat(adaT[:, j, 0:KD, 1:NCOND], NT), ALU.add).then_inc(h_set.sem, 1)

            def residual(j, m, ps, slot, signal):
                t = sq[:, slot, :]
                g = adaT[:, j, ds(2 * KD + m, 1), :].rearrange("p o n -> p (o n)")
                dve.tensor_scalar(t[:, 0:TP], ps[:, 0:TP], g[:, 0:1], None, ALU.mult)
                dve.tensor_tensor(t[:, TP:T].rearrange("p (b t) -> p b t", t=NT),
                                  ps[:, TP:T].rearrange("p (b t) -> p b t", t=NT), repeat(g[:, 1:NCOND], NT), ALU.mult)
                dve.drain()
                x = xT[:, ds(m, 1), :].rearrange("p o t -> p (o t)")
                dve.scalar_tensor_tensor(x, x, ALPHA, t, ALU.mult, ALU.add).then_inc(signal.sem, 1)

            def norm(l, j):
                dve.wait_ge(ln_mean.sem, ln_mean.done(l, j))
                for k in range(KD):
                    dve.tensor_tensor(xT[:, k, :], xT[:, k, :], bank[0][:, 0:T], ALU.subtract).then_inc(ln_xc.sem, 1)
                dve.wait_ge(ln_mm.sem, ln_mm.done(l, KD * j + KD - 1))
                dve.tensor_scalar(rstd[:], bank[1][:, 0:T], EPS, None, ALU.add).then_inc(ln_var.sem, 1)
                dve.wait_ge(ln_std.sem, ln_std.done(l, j))
                dve.reciprocal(rstd[:], rstd[:])
                dve.drain()
                for k in range(KD):
                    dve.tensor_tensor(xT[:, k, :], xT[:, k, :], rstd[:], ALU.mult).then_inc(ln_n.sem, 1)

            def read_logits(l, u):
                dve.wait_ge(u_s.sem, u_s.done(l, u.n))
                dve.wait_ge(u_tp.sem, u_tp.free(l, u.n))
                dve.sem_inc(passed, 1)
                r = u.rows
                bias = {"A": sbiasA, "B": sbiasB, "C": sbiasC}[u.kind]
                dve.tensor_tensor_reduce(out=S[0:r, u.s, :], in0=psf[0:r, 1536 * u.s:1536 * u.s + L], in1=bias[:],
                                         scale=1.0, scalar=-3e38, op0=ALU.add, op1=ALU.max,
                                         accum_out=mx[0:r, u.s, 0:1])
                dve.drain()
                dve.tensor_scalar(nmx[0:r, u.s, 0:1], mx[0:r, u.s, 0:1], -1.0, None, ALU.mult).then_inc(u_logit.sem, 1)

            def read_turned(l, u):
                dve.wait_ge(u_tp.sem, u_tp.done(l, u.n))
                dve.wait_ge(u_o.sem, u_o.free(l, u.n))
                r = u.rows
                dve.tensor_copy(PT[:, u.s, 0:NPG, 0:r], bank[6][:, 0:NPG * r].rearrange("p (j r) -> p j r", r=r))
                dve.tensor_copy(PT[0:NT, u.s, NPG, 0:r], last_keys(u)).then_inc(u_tset.sem, 1)

            def read_outputs(l, u):
                r = u.rows
                dve.wait_ge(u_o.sem, u_o.done(l, u.n))
                dve.reciprocal(rs[0:r, u.s, 0:1], sm[0:r, u.s, 0:1])
                dve.drain()
                src, dst = bank[7][0:r, 0:u.width], osb[0:r, u.s, 0:u.width]
                if u.kind == "C":
                    ins = dve.tensor_scalar(dst, src, rs[0:r, u.s, 0:1], par[0:r, P_COEF:P_COEF + 1], ALU.mult, ALU.mult)
                else:
                    ins = dve.tensor_scalar(dst, src, rs[0:r, u.s, 0:1], None, ALU.mult)
                ins.then_inc(u_oset.sem, 1)

            def place_outputs(l, u):
                dve.wait_ge(u_ot.sem, u_ot.done(l, u.n))
                c0 = outputs_at(u)
                n, gap, m0 = (2, 48, 6) if u.kind == "C" else (3, 64, 0 if u.kind == "A" else 3)
                for half in range(2):
                    q = slice(64 * half, 64 * half + 64)
                    first = psf[q, c0 + NT * half:c0 + NT * half + NT]
                    ins = dve.tensor_copy(oT[q, m0:m0 + n, ds(TP + NT * u.b, NT)],
                                          bass.AP(first.tensor, first.offset, [list(first.ap[0]), [gap, n], [1, NT]]))
                ins.then_inc(u_out.sem, 1)

            def step(l, unit, i, r, prev=True, following=True):
                if prev:
                    read_outputs(l, unit(i, r - 1))
                read_turned(l, unit(i, r))
                if following:
                    read_logits(l, unit(i, r + 1))
                if prev:
                    place_outputs(l, unit(i, r - 1))

            def take8(rows, n):
                for _ in range(n):
                    dve.max(m8[0:rows, 0, :], work[0:rows, :])
                    dve.drain()
                    dve.match_replace(work[0:rows, :], m8[0:rows, 0, :], work[0:rows, :], TAKEN)
                    dve.drain()

            with dve.Fori(0, DEPTH) as l:
                dve.wait_ge(ln_x.sem, ln_x.free(l, 0))
                dve.tensor_copy(par[:], par_all[:, ds(l, 1), :].rearrange("p o n -> p (o n)"))
                dve.drain()
                modulation(l, 0)
                modulate(0)
                modulation(l, 1)
                for g in range(2):
                    dve.wait_ge(tile_used.sem, tile_used.done(l, V_AT + 4 * g + 3))
                    for tt in range(3):
                        dst = vp[:, tt, 512 * g:512 * g + 512] if tt < 2 else vs[:, 512 * g:512 * g + 512]
                        dve.tensor_copy(dst, bank[3 * g + tt][0:P if tt < 2 else TS, :]).then_inc(v_set.sem, 1)
                dve.wait_ge(wi_ps.sem, wi_ps.done(l, 0))
                dve.tensor_copy(wiq[:].rearrange("p a b -> p (a b)"), bank[0][:, 0:2 * HI])
                first = wall[:, 0, 0:NT]
                dve.tensor_tensor(bass.AP(first.tensor, first.offset, [list(first.ap[0]), [TS + NT, NB], [1, NT]]),
                                  bank[0][0:64, 64:128].rearrange("p (b t) -> p b t", t=NT),
                                  tmask[:].rearrange("p (b t) -> p b t", t=NT), ALU.mult).then_inc(wi_set.sem, 1)
                dve.drain()
                for n in range(2 * HI):
                    qt, h = n // HI, n % HI
                    w, at = (P, psel_at[0]) if qt == 0 else (TP, psel_at[1])
                    dve.wait_ge(pd_relu.sem, pd_relu.done(l, n))
                    dve.scalar_tensor_tensor(psc[:, at:at + w], S[:, n % 2, 0:w], wiq[:, qt, h:h + 1],
                                             cmask[:, TP - w:TP] if h == 0 else psc[:, at:at + w], ALU.mult, ALU.add
                                             ).then_inc(pd_acc.sem, 1)
                    dve.drain()
                blocks = [(psel_at[0], P), (psel_at[1], TP)]
                for _ in range(TOPK_P // 8):
                    for e, (at, w) in enumerate(blocks):
                        dve.max(m8[:, e, :], psc[:, at:at + w])
                    dve.drain()
                    for e, (at, w) in enumerate(blocks):
                        dve.match_replace(psc[:, at:at + w], m8[:, e, :], psc[:, at:at + w], TAKEN)
                    dve.drain()
                dve.tensor_scalar(psel[:], psc[:], TAKEN / 2, FAR, ALU.is_gt, ALU.mult).then_inc(psel_set.sem, 1)
                dve.wait_ge(sc_sum.sem, sc_sum.done(l, 0))
                dve.tensor_copy(work[:, 0:PAST], psf[0:TS, 5 * 512:5 * 512 + PAST])
                dve.tensor_tensor(work[:, PAST:L], bank[7][0:TS, 0:NT], smask[:], ALU.add).then_inc(sc_copied.sem, 1)
                dve.drain()
                dve.wait_ge(ld_dist, N_DIST)
                read_logits(l, unit_ac(0, 0))
                step(l, unit_ac, 0, 0, prev=False)
                take8(TS, 2)
                with dve.Fori(0, 3) as i:
                    for r in range(1, 5):
                        step(l, unit_ac, i, r)
                        take8(TS, 2)
                for r in range(1, 4):
                    step(l, unit_ac, 3, r, following=r < 3)
                    take8(TS, 2)
                dve.tensor_scalar(sel[:], work[:], TAKEN / 2, FAR, ALU.is_gt, ALU.mult).then_inc(sel_set.sem, 1)
                read_outputs(l, unit_ac(3, 3))
                place_outputs(l, unit_ac(3, 3))
                read_logits(l, unit_b(0, 0))
                step(l, unit_b, 0, 0, prev=False)
                with dve.Fori(0, 3) as i:
                    for r in range(1, 3):
                        step(l, unit_b, i, r)
                step(l, unit_b, 3, 1, following=False)
                read_outputs(l, unit_b(3, 1))
                place_outputs(l, unit_b(3, 1))

                def item_read(n):
                    qt, g, w, maps = item(n)
                    s = n % 2
                    dve.wait_ge(i_s.sem, i_s.done(l, n))
                    dve.wait_ge(i_tp.sem, i_tp.free(l, n))
                    for e in range(maps // 2):
                        v = slice(2 * w * e, 2 * w * e + 2 * w)
                        first = psf[:, 1024 * s + w * e:1024 * s + w * e + w]
                        ps = bass.AP(first.tensor, first.offset, [list(first.ap[0]), [512, 2], [1, w]])
                        if g < 6:
                            bias = pbias[:, 2 * g:2 * g + 2, TP - w:TP]
                        else:
                            row = pbias[:, HA + HB + 2 * (g - 6) + e, TP - w:TP]
                            bias = bass.AP(row.tensor, row.offset, [list(row.ap[0]), [0, 2], [1, w]])
                        dve.tensor_tensor(S[:, s, v].rearrange("p (m w) -> p m w", w=w),
                                          ps, bias, ALU.add)
                    dve.drain()
                    dve.tensor_reduce(mx[:, s, 0:maps], S[:, s, 0:maps * w].rearrange("p (m w) -> p m w", w=w), AX_X,
                                      ALU.max)
                    dve.drain()
                    dve.tensor_scalar(nmx[:, s, 0:maps], mx[:, s, 0:maps], -1.0, None, ALU.mult
                                      ).then_inc(i_logit.sem, 1)

                def item_out(n):
                    qt, g, w, maps = item(n)
                    dve.wait_ge(i_o.sem, i_o.done(l, n))
                    for e in range(2):
                        q = slice(64 * e, 64 * e + 64)
                        ins = dve.tensor_copy(oT[q, g, P * qt:P * qt + P], bank[6 + n % 2][q, P * e:P * e + P])
                    ins.then_inc(i_out.sem, 1)

                item_read(0)
                for n in range(ITEMS):
                    if n + 1 < ITEMS:
                        item_read(n + 1)
                    qt, g, w, maps = item(n)
                    s = n % 2
                    dve.wait_ge(i_exp.sem, i_exp.done(l, n))
                    dve.reciprocal(rs[:, s, 0:maps], sm[:, s, 0:maps])
                    dve.drain()
                    for e in range(2):
                        m = e if g < 6 else 2 * e
                        v = S[:, s, w * m:w * m + w]
                        ins = dve.tensor_scalar(v, v, rs[:, s, m:m + 1], None, ALU.mult)
                        if g >= 6:
                            dve.tensor_scalar(rs[:, s, m + 1:m + 2], rs[:, s, m + 1:m + 2], par[:, P_NLAM:P_NLAM + 1],
                                              None, ALU.mult)
                    if g >= 6:
                        dve.drain()
                        for m in (0, 2):
                            v, v2 = (S[:, s, w * k:w * k + w] for k in (m, m + 1))
                            ins = dve.scalar_tensor_tensor(v, v2, rs[:, s, m + 1:m + 2], v, ALU.mult, ALU.add)
                    ins.then_inc(i_p.sem, 1)
                    if n:
                        item_out(n - 1)
                item_out(ITEMS - 1)
                dve.drain()
                dve.tensor_tensor(sq[:], oT[:, 6:8, :], oT[:, 6:8, :], ALU.mult).then_inc(gn_sq.sem, 1)
                dve.wait_ge(gn_ps.sem, gn_ps.done(l, 0))
                for c in range(2):
                    ins = dve.tensor_scalar(sq[:, c, :], bank[c][:, 0:T], 1e-5, None, ALU.add)
                ins.then_inc(gn_var.sem, 1)
                dve.wait_ge(gn_std.sem, gn_std.done(l, 0))
                dve.reciprocal(sq[:], sq[:])
                dve.drain()
                dve.tensor_tensor(oT[:, 6:8, :], oT[:, 6:8, :], sq[:], ALU.mult)
                dve.drain()
                dve.tensor_scalar(oT[:, 6:8, :], oT[:, 6:8, :], par[:, P_SUB:P_SUB + 1], None, ALU.mult
                                  ).then_inc(gn_set.sem, 1)
                with dve.Fori(0, WO_T // 2) as i:
                    for m in range(2):
                        dve.wait_ge(tile_used.sem, tile_used.done(l, WO_AT + 2 * i + m))
                        residual(0, 2 * i + m, bank[6 + m], m, wo_set)
                norm(l, 0)
                dve.wait_ge(ln_x.sem, ln_x.done(l, KD - 1))
                modulate(1)
                with dve.Fori(0, UP_T // 2) as i:
                    for k in range(2):
                        dve.wait_ge(up_relu.sem, up_relu.done(l, 2 * i + k))
                        dve.tensor_tensor(uT[:, ds(2 * i + k, 1), :].rearrange("p o t -> p (o t)"), sq[:, k, :],
                                          sq[:, k, :], ALU.mult).then_inc(up_set.sem, 1)
                with dve.Fori(0, KD // 2) as i:
                    for m in range(2):
                        dve.wait_ge(tile_used.sem, tile_used.done(l, DOWN_AT + 8 * i + 4 * m + 3))
                        residual(1, 2 * i + m, bank[6 + m], m, dn_set)
                norm(l, 1)


def bucket(dist):
    exact, n_buckets, far = 16, 32, 128
    n = max(dist, 0)
    if n < exact:
        return n
    return min(exact + int(math.log(n / exact) / math.log(far / exact) * (n_buckets - exact)), n_buckets - 1)


def constants():
    dist = DIST0 - np.arange(NDIST)
    onehot = np.zeros((34, NDIST), np.float32)
    onehot[[bucket(d) for d in dist], np.arange(NDIST)] = 1
    held = np.zeros(NDIST)
    for win, dil in ((128, 1), (512, 4), (2048, 16)):
        held += (dist >= 0) & (dist <= win) & (dist % dil == 0)
    onehot[32] = np.where(held > 0, np.log(np.maximum(held, 1)), FAR)
    onehot[33] = np.where(dist >= 0, 0, FAR)
    relrows = np.zeros((2, H), np.float32)
    relrows[0, :HA] = 1
    relrows[1, HA:] = 1
    zscale = np.ones((P, NZ), np.float32)
    zscale[:, QI:QC] = DH ** -0.5
    zscale[:, QC:KA] = DC ** -0.5
    hd = np.arange(P) // DH
    ht = np.arange(HI * NT)
    bt = np.arange(TS)
    selB = np.zeros((TS, NB, RA), np.float32)
    for b in range(NB):
        for r in range(RA):
            selB[b * NT + r % NT, b, r] = 1
    sumC = np.zeros((RC, 32), np.float32)
    for r in range(RC):
        sumC[r, r // 16 * NT + r % NT] = 1
    is1 = ((np.arange(P) // NT) % 2 == 1).astype(np.float32)
    p, j = np.arange(P)[:, None], np.arange(TP)[None]
    t, u = np.arange(TS)[:, None] % NT, np.arange(NT)[None]
    f, bf = np.float32, mybir.dt.np(BF16)
    return {
        "ident": np.eye(P, dtype=f), "ident16": np.eye(P).astype(bf),
        "onesd": np.full((P, P), 1 / D, f), "oneshd": ((hd[:, None] == hd[None]) / DH).astype(f),
        "zscale": zscale, "relrows": relrows, "onehot": onehot,
        "rep": (np.arange(HI)[:, None] == ht[None] // NT).astype(f),
        "tmask": (ht[:, None] % NT == bt[None] % NT).astype(f),
        "selB": selB.astype(bf), "sumC": sumC, "ismap1": np.stack([is1, 1 - is1], 1),
        "cmask": np.where(P + p - j >= 0, 0, FAR).astype(f), "smask": np.where(t >= u, 0, FAR).astype(f),
    }


def kernel(**inputs):
    import concourse.bacc as bacc
    from concourse.bass_utils import run_bass_kernel_spmd

    v = {k: np.asarray(x) for k, x in inputs.items()}

    def narrow(w):
        return w.reshape(-1, KD, P, w.shape[1] // P, P).transpose(3, 0, 2, 1, 4).reshape(-1, P, KD * P)

    def wide(w):
        return w.reshape(4, 2, P, w.shape[1] // 512, 512).transpose(3, 0, 2, 1, 4).reshape(-1, P, KD * P)

    names = ("qa", "ka", "va", "qb", "kb", "vb", "qi", "ki", "wi", "qc", "kc", "vc")
    sizes = (384, 384, 384, 384, 384, 384, 512, 64, 8, 256, 256, 256)
    at = dict(zip(names, np.cumsum((0,) + sizes[:-1])))
    tiles, wki = [], []
    for l in range(DEPTH):
        part = {n: v["w_in"][l][:, at[n]:at[n] + s] for n, s in zip(names, sizes)}
        tiles += [wide(v["w_ada_mix"][l]), wide(v["w_ada_mlp"][l]),
                  wide(np.concatenate([part[n] for n in ("va", "vb", "vc")], 1)),
                  narrow(np.concatenate([part[n] for n in ("qi", "qa", "qb", "qc", "ka", "kb", "kc")], 1)),
                  narrow(v["w_o"][l]), narrow(v["w_up"][l]), narrow(v["w_down"][l])]
        w = np.concatenate([part["ki"], part["ki"], part["wi"]], 1)
        wki.append(w.reshape(KD, P, -1).transpose(1, 0, 2))

    def pages(k, val):
        n, _, f = k.shape
        kt = k.transpose(0, 2, 1).reshape(n, f // P, P, PAGE).transpose(0, 2, 1, 3).reshape(n, P, f)
        return np.concatenate([kt, val], 2)

    n_pool = DEPTH * N_PHYS
    ca = pages(v["cache_a_k"].reshape(DEPTH * NB * NPG, P, 384), v["cache_a_v"].reshape(DEPTH * NB * NPG, P, 384))
    chunk = lambda x: x.reshape(x.shape[:-1] + (-1, P))
    cols = lambda x: np.moveaxis(chunk(x), -1, 0)
    params = np.concatenate([
        cols(v["b_ada_mix"]), cols(v["b_ada_mlp"]), cols(v["ln1_g"]), cols(v["ln1_b"]), cols(v["ln2_g"]),
        cols(v["ln2_b"]), np.tile(v["subln_g"], (1, 2)).T[:, :, None]], 2)
    xs = np.concatenate([v["x_prompt"].reshape(TP, D), v["x_sample"].reshape(TS, D)])
    cond = np.concatenate([v["c_prompt"], v["c_sample"]])
    arrays = {
        "x": xs.reshape(T, KD, P).transpose(2, 1, 0), "cond": cond.reshape(NCOND, KD, P).transpose(2, 1, 0),
        "rel_bias": v["rel_bias"], "lam": v["lam"].reshape(1, -1), "page_table": v["page_table"].reshape(1, -1),
        "params": params, "tiles": np.concatenate(tiles), "wki": np.stack(wki),
        "cache_a": ca.reshape(DEPTH * NB, NPG, P, AB_W).transpose(0, 2, 1, 3).reshape(DEPTH * NB, P, -1),
        "pool_b": pages(v["cache_b_k"].reshape(n_pool, P, 384), v["cache_b_v"].reshape(n_pool, P, 384)),
        "pool_c": pages(v["cache_c_k"].reshape(n_pool, P, 256), v["cache_c_v"].reshape(n_pool, P, 256)),
        "pool_ik": v["cache_b_ik"].reshape(n_pool, P, DH).transpose(0, 2, 1),
        **constants(),
    }
    shapes = {"y": (P, KD, T), "z": (DEPTH, P, KI + 1 - KA, T), "vp": (DEPTH, P, 2, D), "vs": (DEPTH, TS, D),
              "cache_a": (DEPTH * NB, P, NPG * AB_W)}
    nc = bacc.Bacc("TRN2", target_bir_lowering=False, num_devices=1, dynamic_dma_scratch_size=1024)
    ins, feeds = {}, {}
    for name, x in arrays.items():
        x = np.ascontiguousarray(x)
        feeds[f"in_{name}"] = x
        ins[name] = nc.dram_tensor(f"in_{name}", x.shape, mybir.dt.from_np(x.dtype), kind="ExternalInput").ap()
    outs = {n: nc.dram_tensor(f"out_{n}", s, F32, kind="ExternalOutput").ap() for n, s in shapes.items()}
    program(nc, ins, outs)
    r = run_bass_kernel_spmd(nc, [feeds], core_ids=[0]).results[0]
    got = {n: np.asarray(r[f"out_{n}"]).reshape(s) for n, s in shapes.items()}

    y = got["y"].transpose(2, 1, 0).reshape(T, D)
    z = got["z"].transpose(0, 3, 2, 1).reshape(DEPTH, T, -1)
    ka, kb, kc, ki = z[..., 0:384], z[..., 384:768], z[..., 768:1024], z[..., 1024:1024 + DH]
    vpr = got["vp"].transpose(0, 2, 1, 3).reshape(DEPTH, TP, D)
    vsm = got["vs"]
    c = got["cache_a"].reshape(DEPTH, NB, P, NPG, AB_W)
    c_k = c[..., 0:384].reshape(DEPTH, NB, P, NPG, 3, P).transpose(0, 1, 3, 5, 4, 2).reshape(DEPTH, NB, PAST, 384)
    c_v = c[..., 384:].transpose(0, 1, 3, 2, 4).reshape(DEPTH, NB, PAST, 384)
    pr = lambda x, *s: np.ascontiguousarray(x).reshape(DEPTH, 1, TP, *s)
    sm = lambda x, *s: np.ascontiguousarray(x).reshape(DEPTH, NB, NT, *s)
    p, s = slice(0, TP), slice(TP, T)
    new_k = np.concatenate([c_k.reshape(DEPTH, NB, PAST, HA, DH), sm(ka[:, s], HA, DH)], 2)
    new_v = np.concatenate([c_v.reshape(DEPTH, NB, PAST, HA, DH), sm(vsm[..., VA:VB], HA, DH)], 2)
    return (y[p].reshape(1, TP, D).copy(), y[s].reshape(NB, NT, D).copy(),
            pr(ka[:, p], HA, DH), pr(vpr[..., VA:VB], HA, DH), pr(kb[:, p], HB, DH), pr(vpr[..., VB:VC], HB, DH),
            pr(ki[:, p], DH), pr(kc[:, p], HC, 2, DC), pr(vpr[..., VC:], HC, 2 * DC),
            new_k, new_v, sm(kb[:, s], HB, DH), sm(vsm[..., VB:VC], HB, DH), sm(ki[:, s], DH),
            sm(kc[:, s], HC, 2, DC), sm(vsm[..., VC:], HC, 2 * DC))
```

```python
import math
from contextlib import ExitStack

import numpy as np

import concourse.bass as bass
from concourse import mybir

F32 = mybir.dt.float32
BF16 = mybir.dt.bfloat16
I32 = mybir.dt.int32
ALU = mybir.AluOpType
ACT = mybir.ActivationFunctionType
AX_X = mybir.AxisListType.X
ds = bass.ds

P = 128
D = 1024
KD = D // P
DEPTH = 2
TP = 256
NB = 8
NT = 8
TS = NB * NT
T = TP + TS
PAST = 1024
L = PAST + NT
PAGE = 128
NPG = PAST // PAGE
N_PHYS = 80
HA = HB = 6
HC = 4
HI = 8
H = HA + HB + HC
DH = 64
DC = 32
FF = 4096
NCOND = 1 + NB
TOPK_P = min(256, TP // 4)
TOPK_S = min(256, L // 4)
ALPHA = (2 * DEPTH) ** 0.25
EPS = 1e-5
FAR = -1e30
TAKEN = -3e38
LAM_INIT = [0.8 - 0.6 * math.exp(-0.3 * l) for l in range(DEPTH)]

QI, QA, QB, QC, KA, KB, KC, KI, WI = 0, 4, 7, 10, 12, 15, 18, 20, 21
NZ = 22
VA, VB, VC = 0, 384, 768

ADA_T, V_T, FEAT_T, WO_T, UP_T, DOWN_T = 24, 8, 20, 8, 32, 32
RING = 4
V_AT = ADA_T
FEAT_AT = V_AT + V_T
ADA2_AT = FEAT_AT + FEAT_T
WO_AT = ADA2_AT + ADA_T
UP_AT = WO_AT + WO_T
DOWN_AT = UP_AT + UP_T
TILES = DOWN_AT + DOWN_T

DIST0 = L - 1
NDIST = DIST0 + P
NEAR0 = DIST0 - TP + 1
NEAR_W = NDIST - NEAR0 + 1

G = 32
RA, RC = 3 * G, 2 * G
A_W = NPG * HA * DH
C_W = NPG * HC * DH
AC_UNITS, UNITS = 2 * NB, 3 * NB
ITEMS = 16
ADA_ITEMS = ADA_T // 2
ADA_FROM = 3
A_LOADS = 4 * 16
AB_LOADS = A_LOADS + 4 * NPG * 16
PAGES = NPG * 16
IK_SLOTS = 4

P_ADA, P_LN, P_SUB, P_NLAM, P_COEF = 0, 48, 80, 81, 82
NPAR = 83


class Signal:

    def __init__(self, sem, per, spare=0):
        self.sem, self.per, self.spare = sem, per, spare

    def done(self, l, n):
        return l * self.per + (n + 1 + self.spare)

    def free(self, l, n):
        return l * self.per + (n + 1)


class Unit:

    def __init__(self, n, kind, b, s, v, nth):
        self.n, self.kind, self.b, self.s, self.v, self.nth = n, kind, b, s, v, nth
        self.rows = RC if kind == "C" else RA
        self.chunks = 2 if kind == "C" else 3
        self.held = G if kind == "C" else 2 * NT
        self.v0 = {"A": VA, "B": VB, "C": VC}[kind]


def unit_ac(i, r):
    return Unit(4 * i + r, "AC"[r % 2], 2 * i + r // 2, r % 2, r // 2 % 2, i + r // 4)


def unit_b(i, r):
    return Unit(AC_UNITS + 2 * i + r, "B", 2 * i + r, r % 2, r % 2, i + r // 2)


def item(n):
    qt, g = n // 8, n % 8
    return qt, g, (P if qt == 0 else TP), (2 if g < 6 else 4)


def repeat(ap, n):
    return bass.AP(ap.tensor, ap.offset, [*[list(x) for x in ap.ap], [0, n]])


def program(nc, a, out):
    ctx = ExitStack()
    with ctx:
        def sb(name, shape, dt=F32):
            return ctx.enter_context(nc.sbuf_tensor(name, shape, dt))

        def sem(name):
            return ctx.enter_context(nc.semaphore(name))

        xT = sb("xT", [P, KD, T])
        hT = sb("hT", [P, KD, T])
        oT = hT
        zT = sb("zT", [P, NZ, T])
        vp = sb("vp", [P, 2, D])
        vs = sb("vs", [TS, D])
        vnew = sb("vnew", [NT, 2, D])
        pbias = sb("pbias", [P, H, TP])
        sbiasA = sb("sbiasA", [RA, L])
        sbiasB = sb("sbiasB", [RA, L])
        sbiasC = sb("sbiasC", [RC, L])
        ring = sb("ring", [P, RING, KD, P])
        wki = sb("wki", [P, KD, P + HI])
        big = sb("big", [P, 2 * 2 * A_W])
        ab = big[:, :].rearrange("p (s h j w) -> p s h j w", s=2, h=2, j=NPG)
        uT = big[:, 0:FF // P * T].rearrange("p (m t) -> p m t", t=T)
        cbuf = sb("cbuf", [P, 2 * C_W])
        cs = cbuf[:, :].rearrange("p (h j w) -> p h j w", h=2, j=NPG)
        ik = cbuf[:, 0:IK_SLOTS * NPG * P].rearrange("p (s j w) -> p s j w", s=IK_SLOTS, j=NPG)
        adarow = cbuf[:, 0:6 * P]
        onehot = big[0:34, 0:NDIST]
        distb = big[0:H, 2048:2048 + NDIST]
        qab = sb("qab", [P, 2, RA])
        qc = sb("qc", [P, RC])
        qi = sb("qi", [P, 2, HI * NT])
        wall = sb("wall", [HI * NT, NB, TS])
        S = sb("S", [P, 2, L])
        PT = sb("PT", [P, 2, 9, 64])
        osb = sb("osb", [RA, 2, P])
        work = sb("work", [TS, L])
        sel = sb("sel", [P, L], BF16)
        psc = sb("psc", [P, 384])
        psel = sb("psel", [P, 384], BF16)
        adaT = sb("adaT", [P, 2, 24, NCOND])
        par_all = sb("par_all", [P, DEPTH, NPAR])
        par = sb("par", [P, NPAR])
        sq = sb("sq", [P, 2, T])
        rstd = sb("rstd", [P, T])
        tmp = sq[:, 0, :]
        ident = sb("ident", [P, P])
        ident16 = sb("ident16", [P, P], BF16)
        onesd = sb("onesd", [P, P])
        oneshd = sb("oneshd", [P, P])
        zscale = sb("zscale", [P, NZ])
        cT = sb("cT", [P, KD, NCOND])
        sgm = sb("sgm", [P, KD, NCOND])
        cz = sb("cz", [P, KD, G])
        relb = sb("relb", [34, H])
        rep = sb("rep", [HI, HI * NT])
        tmask = sb("tmask", [HI * NT, TS])
        selB = sb("selB", [TS, NB, G], BF16)
        sumC = sb("sumC", [RC, 32])
        ismap1 = sb("ismap1", [P, 2])
        zero16 = sb("zero16", [P, 512], BF16)
        epsc = sb("epsc", [P, 1])
        wcur = sb("wcur", [HI * NT, 2, TS])
        kin = sb("kin", [P, 2, NT])
        selcur = sb("selcur", [P, 2, G], BF16)
        knew = sb("knew", [P, 2, 3, NT])
        smask = sb("smask", [TS, NT])
        lamb = S[:, 0, 0:DEPTH * 4 * DC].rearrange("p (l a d) -> p l a d", l=DEPTH, a=4)
        lp = S[:, 1, 0:DEPTH * 2 * DC].rearrange("p (e d) -> p e d", d=DC)
        ls = sb("ls", [P, DEPTH * 2])
        cmask = sb("cmask", [P, TP])
        ptab = sb("ptab", [1, NB * NPG], I32)
        wiq = sb("wiq", [P, 2, HI])
        m8 = sb("m8", [P, 2, 8])
        mx = sb("mx", [P, 2, 4])
        nmx = sb("nmx", [P, 2, 4])
        sm = sb("sm", [P, 2, 4])
        rs = sb("rs", [P, 2, 4])
        PTf = PT[:, :, :, :].rearrange("p s j r -> p s (j r)")
        psel_at = [TP, 0]
        dist_s = nc.dram_tensor("dist_sample", [H, NT, NDIST], F32, kind="Internal").ap()
        dist_p = nc.dram_tensor("dist_prompt", [P, H, NEAR_W], F32, kind="Internal").ap()

        psf = ctx.enter_context(nc.psum_tensor("psf", [P, 8 * 512], F32))
        bank = [psf[:, 512 * i:512 * i + 512] for i in range(8)]

        passed = sem("passed")
        ld_const = sem("ld_const")
        ld_w = [sem(f"ld_w{s}") for s in range(RING)]
        ld_wki = sem("ld_wki")
        ld_ik = [sem(f"ld_ik{s}") for s in range(IK_SLOTS)]
        ld_abk = [sem(f"ld_abk{s}") for s in range(2)]
        ld_abv = [sem(f"ld_abv{s}") for s in range(2)]
        ld_ck = sem("ld_ck")
        ld_cv = sem("ld_cv")
        ld_vnew = [sem(f"ld_vnew{s}") for s in range(2)]
        ld_dist = sem("ld_dist")
        st_dist = sem("st_dist")
        st_a = sem("st_a")
        st_state = sem("st_state")
        st_y = sem("st_y")
        zeroed = sem("zeroed")
        dist_ps = sem("dist_ps")
        dist_sb = sem("dist_sb")
        sig_exp = sem("sig_exp")
        silu_done = sem("silu_done")
        lam_sum = sem("lam_sum")
        lam_exp = sem("lam_exp")
        tile_used = Signal(sem("tile_used"), TILES, RING)
        ada_row = Signal(sem("ada_row"), 6, 2)
        ada_row2 = Signal(sem("ada_row2"), 6, 1)
        ada_tp = Signal(sem("ada_tp"), 2)
        ada_set = Signal(sem("ada_set"), 2)
        h_prompt = Signal(sem("h_prompt"), 2 * KD)
        h_sample = Signal(sem("h_sample"), 2 * KD)
        v_set = Signal(sem("v_set"), 6)
        z_ps = Signal(sem("z_ps"), 2)
        z_set = Signal(sem("z_set"), NZ, 2)
        wi_ps = Signal(sem("wi_ps"), 1)
        wi_set = Signal(sem("wi_set"), 1)
        pd_ps = Signal(sem("pd_ps"), 2 * HI)
        pd_relu = Signal(sem("pd_relu"), 2 * HI, 2)
        pd_acc = Signal(sem("pd_acc"), 2 * HI, 2)
        psel_set = Signal(sem("psel_set"), 1)
        qi_set = Signal(sem("qi_set"), NB)
        sd_ps = Signal(sem("sd_ps"), NB)
        sd_relu = Signal(sem("sd_relu"), NB, 2)
        sc_ps = Signal(sem("sc_ps"), NB, 2)
        sc_sum = Signal(sem("sc_sum"), 1)
        sc_copied = Signal(sem("sc_copied"), 1)
        sel_set = Signal(sem("sel_set"), 1)
        q_set = Signal(sem("q_set"), UNITS)
        u_s = Signal(sem("u_s"), UNITS, 2)
        u_logit = Signal(sem("u_logit"), UNITS, 2)
        u_exp = Signal(sem("u_exp"), UNITS)
        u_tp = Signal(sem("u_tp"), UNITS, 2)
        u_tset = Signal(sem("u_tset"), UNITS, 1)
        u_o = Signal(sem("u_o"), UNITS, 2)
        u_oset = Signal(sem("u_oset"), UNITS, 1)
        u_ot = Signal(sem("u_ot"), UNITS)
        u_out = Signal(sem("u_out"), UNITS, 2)
        i_s = Signal(sem("i_s"), ITEMS)
        i_logit = Signal(sem("i_logit"), ITEMS, 2)
        i_exp = Signal(sem("i_exp"), ITEMS)
        i_p = Signal(sem("i_p"), ITEMS)
        i_tp = Signal(sem("i_tp"), ITEMS, 2)
        i_tset = Signal(sem("i_tset"), ITEMS, 2)
        i_o = Signal(sem("i_o"), ITEMS, 2)
        i_out = Signal(sem("i_out"), ITEMS, 1)
        gn_sq = Signal(sem("gn_sq"), 1)
        gn_ps = Signal(sem("gn_ps"), 1)
        gn_std = Signal(sem("gn_std"), 1)
        gn_set = Signal(sem("gn_set"), 1)
        wo_set = Signal(sem("wo_set"), KD, 2)
        dn_set = Signal(sem("dn_set"), KD, 2)
        ln_mean = Signal(sem("ln_mean"), 2)
        ln_xc = Signal(sem("ln_xc"), 2 * KD)
        ln_sq = Signal(sem("ln_sq"), 2 * KD)
        ln_mm = Signal(sem("ln_mm"), 2 * KD, 2)
        ln_std = Signal(sem("ln_std"), 2)
        ln_n = Signal(sem("ln_n"), 2 * KD)
        ln_x = Signal(sem("ln_x"), 2 * KD, 1)
        up_relu = Signal(sem("up_relu"), FF // P, 2)
        up_set = Signal(sem("up_set"), FF // P, 2)

        def turned_at(u, j):
            if j == NPG:
                return 1536 * u.s + 1024 + 304
            n = 512 // u.rows
            return 6 * 512 + u.rows * j if j < n else 1536 * u.s + 1024 + 16 + u.rows * (j - n)

        def outputs_at(u):
            return 1536 * (1 - u.s) + 1024 + 400

        block = ctx.enter_context(nc.Block())

        consts = [(xT[:], a["x"]), (ident[:], a["ident"]), (ident16[:], a["ident16"]), (onesd[:], a["onesd"]),
                  (oneshd[:], a["oneshd"]), (zscale[:], a["zscale"]), (cT[:], a["cond"]),
                  (relb[0:32, :], a["rel_bias"]), (relb[32:34, :], a["relrows"]), (onehot, a["onehot"]),
                  (rep[:], a["rep"]), (tmask[:], a["tmask"]), (selB[:], a["selB"]), (sumC[:], a["sumC"]),
                  (ismap1[:], a["ismap1"]), (cmask[:], a["cmask"]), (smask[:], a["smask"]),
                  (ptab[:], a["page_table"]), (par_all[:, :, 0:P_NLAM], a["params"])]
        N_CONST = 16 * (len(consts) + 1)
        N_DIST = 16 * (2 * 3 + 2 * HC + 1)

        @block.sync
        def _(sp):
            for dst, src in consts:
                sp.dma_start(dst, src).then_inc(ld_const, 16)
            sp.dma_start(S[:, 0, 0:DEPTH * 4 * DC], a["lam"].to_broadcast([P, DEPTH * 4 * DC])
                         ).then_inc(ld_const, 16)
            def four_tiles(l, at):
                for s in range(RING):
                    sp.wait_ge(tile_used.sem, tile_used.free(l, at + s))
                    sp.dma_start(ring[:, s].rearrange("p k m -> p (k m)"),
                                 a["tiles"][ds(l * TILES + at + s, 1)].rearrange("o p w -> (o p) w")
                                 ).then_inc(ld_w[s], 16)

            def tiles(l, at, n, copies=None):
                sp.sem_inc(passed, 1)
                with sp.Fori(0, n // RING) as i:
                    four_tiles(l, at + RING * i)
                    if copies is not None:
                        p0 = 16 * copies
                        sp.dma_start(out["cache_a"][ds(l * NB + i, 1), p0:p0 + 64, :].rearrange("o p w -> (o p) w"),
                                     a["cache_a"][ds(l * NB + i, 1), p0:p0 + 64, :].rearrange("o p w -> (o p) w")
                                     ).then_inc(st_a, 16)

            def load_a(l, b, s, half):
                sp.dma_start(ab[:, s, half].rearrange("p j w -> p (j w)"),
                             a["cache_a"][ds(l * NB + b, 1), :, half * A_W:(half + 1) * A_W]
                             .rearrange("o p w -> (o p) w")).then_inc((ld_abk, ld_abv)[half][s], 16)

            def load_pages(l, b, pool, dst, signal):
                sp.sem_inc(passed, 1)
                _, at = nc.values_load_multi_w_load_instructions(ptab[0:1, ds(b * NPG, NPG)], [mybir.EngineType.SP],
                                                                 min_val=0, max_val=N_PHYS - 1)
                for j in range(NPG):
                    sp.dma_start(dst[:, j, :], pool[ds(at[j] + l * N_PHYS, 1)].rearrange("o p w -> (o p) w")
                                 ).then_inc(signal, 16)

            def load_b(l, b, s, half):
                load_pages(l, b, a["pool_bv" if half else "pool_bk"], ab[:, s, half], (ld_abk, ld_abv)[half][s])

            def load_c(l, b, half):
                load_pages(l, b, a["pool_cv" if half else "pool_ck"], cs[:, half], (ld_ck, ld_cv)[half])

            def load_ik(l, b, s):
                load_pages(l, b, a["pool_ik"], ik[:, s], ld_ik[s])

            def load_vnew(l, b, s):
                sp.dma_start(vnew[:, s, :], out["vs"][ds(l, 1), ds(b * NT, NT), :].rearrange("o t w -> (o t) w")
                             ).then_inc(ld_vnew[s], 16)

            with sp.Fori(0, DEPTH) as l:
                tiles(l, 0, ADA_T)
                tiles(l, V_AT, V_T)
                sp.wait_ge(ada_tp.sem, ada_tp.done(l, 0))
                sp.wait_ge(st_dist, 32)
                for i in range(FEAT_T // RING):
                    four_tiles(l, FEAT_AT + RING * i)
                    if i < IK_SLOTS:
                        load_ik(l, i, i)
                        load_a(l, i // 2, i // 2, i % 2)
                    if i == 2:
                        sp.dma_start(wki[:], a["wki"][ds(l, 1)].rearrange("o p k m -> (o p) k m")
                                     ).then_inc(ld_wki, 16)
                sp.wait_ge(v_set.sem, v_set.done(l, 5))
                sp.dma_start(out["vs"][ds(l, 1)].rearrange("o p t -> (o p) t"), vs[:]).then_inc(st_state, 16)
                sp.dma_start(out["vp"][ds(l, 1)].rearrange("o p k t -> (o p) k t"), vp[:]).then_inc(st_state, 16)
                sp.wait_ge(st_state, 48 * l + 32)
                for b in range(2):
                    load_vnew(l, b, b)
                sp.wait_ge(z_set.sem, z_set.done(l, NZ - 1))
                sp.dma_start(out["z"][ds(l, 1)].rearrange("o p k t -> (o p) k t"), zT[:, KA:KI + 1, :]
                             ).then_inc(st_state, 16)
                for b in range(IK_SLOTS, NB):
                    sp.wait_ge(sd_ps.sem, sd_ps.done(l, b - IK_SLOTS))
                    load_ik(l, b, b - IK_SLOTS)
                sp.wait_ge(sd_ps.sem, sd_ps.done(l, NB - 1))
                load_c(l, 0, 0)
                load_c(l, 0, 1)
                four_tiles(l, ADA2_AT)
                with sp.Fori(0, 3) as i:
                    for s in range(2):
                        b = 2 * i + s
                        sp.wait_ge(u_s.sem, u_s.done(l, 4 * i + 2 * s + 1))
                        load_c(l, b + 1, 0)
                        load_a(l, b + 2, s, 0)
                        sp.wait_ge(u_o.sem, u_o.done(l, 4 * i + 2 * s))
                        load_a(l, b + 2, s, 1)
                        sp.wait_ge(u_o.sem, u_o.done(l, 4 * i + 2 * s + 1))
                        load_c(l, b + 1, 1)
                        load_vnew(l, b + 2, s)
                for s in range(2):
                    b = NB - 2 + s
                    sp.wait_ge(u_s.sem, u_s.done(l, 2 * b + 1))
                    if s == 0:
                        load_c(l, b + 1, 0)
                    load_b(l, s, s, 0)
                    sp.wait_ge(u_o.sem, u_o.done(l, 2 * b))
                    load_b(l, s, s, 1)
                    sp.wait_ge(u_o.sem, u_o.done(l, 2 * b + 1))
                    if s == 0:
                        load_c(l, b + 1, 1)
                    load_vnew(l, s, s)

                def next_keys(n, b, s):
                    sp.wait_ge(u_s.sem, u_s.done(l, n))
                    load_b(l, b + 2, s, 0)

                def next_values(n, b, s):
                    sp.wait_ge(u_o.sem, u_o.done(l, n))
                    load_b(l, b + 2, s, 1)
                    load_vnew(l, b + 2, s)

                next_keys(AC_UNITS, 0, 0)
                with sp.Fori(0, 2) as i:
                    for s in range(2):
                        next_keys(AC_UNITS + 2 * i + s + 1, 2 * i + s + 1, 1 - s)
                        next_values(AC_UNITS + 2 * i + s, 2 * i + s, s)
                next_keys(AC_UNITS + 5, 5, 1)
                for s in range(2):
                    next_values(AC_UNITS + 4 + s, 4 + s, s)
                tiles(l, ADA2_AT + RING, ADA_T - RING)
                tiles(l, WO_AT, WO_T)
                tiles(l, UP_AT, UP_T, 0)
                sp.wait_ge(st_state, 48 * l + 48)
                tiles(l, DOWN_AT, DOWN_T, 4)
            for k in range(1, KD, 2):
                sp.wait_ge(ln_x.sem, ln_x.done(DEPTH - 1, KD + k))
                sp.dma_start(out["y"][:, k - 1:k + 1, :], xT[:, k - 1:k + 1, :]).then_inc(st_y, 16)
            sp.wait_ge(st_y, KD // 2 * 16)
            sp.wait_ge(st_a, DEPTH * 2 * NB * 16)
            sp.wait_ge(st_state, 48 * DEPTH)

        @block.gpsimd
        def _(pool):
            for t in (cz, qab, qc, qi, wall, zero16, sel, selcur, sbiasA, sbiasB):
                pool.memset(t[:], 0.0)
            pool.memset(epsc[:], EPS)
            pool.drain()
            pool.sem_inc(zeroed, 1)

            def modulate_sample(l, j, k):
                hs = hT[:, k, TP:T].rearrange("p (b t) -> p b t", t=NT)
                pool.tensor_tensor(hs, xT[:, k, TP:T].rearrange("p (b t) -> p b t", t=NT),
                                   repeat(adaT[:, j, KD + k, 1:NCOND], NT), ALU.mult)
                pool.drain()
                pool.tensor_tensor(hs, hs, repeat(adaT[:, j, k, 1:NCOND], NT), ALU.add).then_inc(h_sample.sem, 1)

            with pool.Fori(0, DEPTH) as l:
                pool.wait_ge(ada_set.sem, ada_set.done(l, 0))
                for k in range(KD):
                    modulate_sample(l, 0, k)
                pool.wait_ge(z_set.sem, z_set.done(l, NZ - 1))
                pool.wait_ge(wi_set.sem, wi_set.done(l, 0))
                pool.sem_inc(passed, 1)
                with pool.Fori(0, NB // 2) as i:
                    for s in range(2):
                        pool.wait_ge(sc_ps.sem, sc_ps.free(l, 2 * i + s))
                        for half in range(2):
                            q = slice(64 * half, 64 * half + 64)
                            pool.tensor_copy(qi[q, s, :].rearrange("p (c e t) -> p c e t", e=2, t=NT)[:, :, half, :],
                                             zT[q, QI:QI + 4, ds(TP + NT * (2 * i + s), NT)])
                            pool.drain()
                        pool.tensor_copy(kin[:, s, :], zT[:, KI, ds(TP + NT * (2 * i + s), NT)])
                        pool.drain()
                        pool.tensor_copy(wcur[:, s, :], wall[:, ds(2 * i + s, 1), :].rearrange("p o t -> p (o t)"))
                        pool.drain()
                        pool.sem_inc(qi_set.sem, 1)

                def queries(u):
                    pool.wait_ge(u_s.sem, u_s.free(l, u.n))
                    if u.kind == "C":
                        for g in range(4):
                            q = slice(32 * g, 32 * g + 32)
                            first = qc[q, NT * g:NT * g + NT]
                            pool.tensor_copy(bass.AP(first.tensor, first.offset, [list(first.ap[0]), [G, 2], [1, NT]]),
                                             zT[q, QC:QC + 2, ds(TP + NT * u.b, NT)])
                            pool.drain()
                    else:
                        c0, s = (QA, 0) if u.kind == "A" else (QB, u.s)
                        for half in range(2):
                            q = slice(64 * half, 64 * half + 64)
                            first = qab[q, s, NT * half:NT * half + NT]
                            pool.tensor_copy(bass.AP(first.tensor, first.offset, [list(first.ap[0]), [G, 3], [1, NT]]),
                                             zT[q, c0:c0 + 3, ds(TP + NT * u.b, NT)])
                            pool.drain()
                        if u.kind == "B":
                            pool.tensor_copy(selcur[0:TS, s, :], selB[:, ds(u.b, 1), :].rearrange("p o r -> p (o r)"))
                    k0 = {"A": KA, "B": KB, "C": KC}[u.kind]
                    pool.tensor_copy(knew[:, u.s, 0:u.chunks, :], zT[:, k0:k0 + u.chunks, ds(TP + NT * u.b, NT)])
                    pool.drain()
                    pool.sem_inc(q_set.sem, 1)

                with pool.Fori(0, NB // 2) as i:
                    for r in range(4):
                        queries(unit_ac(i, r))
                with pool.Fori(0, NB // 2) as i:
                    for r in range(2):
                        queries(unit_b(i, r))
                for k in range(KD):
                    pool.wait_ge(ln_x.sem, ln_x.done(l, k))
                    modulate_sample(l, 1, k)

        @block.scalar
        def _(act):
            for signal in (ada_row, ada_row2, z_set, pd_relu, sd_relu, i_tset, up_relu, ln_x):
                act.sem_inc(signal.sem, signal.spare)
            act.wait_ge(ld_const, N_CONST)
            act.activation(sgm[:], cT[:], ACT.Exp, scale=-1.0).then_inc(sig_exp, 1)
            act.wait_ge(lam_sum, 1)
            act.activation(ls[:], ls[:], ACT.Exp).then_inc(lam_exp, 1)
            act.wait_ge(dist_sb, 3)
            act.dma_start(dist_s.rearrange("h t u -> h t u"), bass.AP(distb.tensor, distb.offset,
                          [list(distb.ap[0]), [0, NT], [1, NDIST]])).then_inc(st_dist, 16)
            near = distb[:, NEAR0:NDIST]
            act.dma_start(dist_p[:, :, 0:NDIST - NEAR0].rearrange("p h u -> h p u"), bass.AP(near.tensor, near.offset,
                          [list(near.ap[0]), [0, P], [1, NDIST - NEAR0]])).then_inc(st_dist, 16)
            act.wait_ge(st_dist, 32)
            row = NT * NDIST
            act.wait_ge(zeroed, 1)
            for dst, h0 in ((sbiasA, 0), (sbiasB, HA)):
                for c in range(3):
                    act.dma_start(dst[G * c:G * c + 2 * NT, :],
                                  bass.AP(dist_s.tensor, (h0 + 2 * c) * row + NT - 1, [[row, 2], [NDIST - 1, NT], [1, L]])
                                  ).then_inc(ld_dist, 16)
            for r in range(2 * HC):
                act.dma_start(sbiasC[r * NT:r * NT + NT, :],
                              bass.AP(dist_s.tensor, (HA + HB + r // 2) * row + NT - 1, [[NDIST - 1, NT], [1, L]])
                              ).then_inc(ld_dist, 16)
            act.dma_start(pbias[:], bass.AP(dist_p.tensor, DIST0 - P - NEAR0,
                                            [[H * NEAR_W - 1, P], [NEAR_W, H], [1, TP]])).then_inc(ld_dist, 16)
            with act.Fori(0, DEPTH) as l:
                with act.Fori(0, 3) as i:
                    for k in range(2):
                        act.wait_ge(tile_used.sem, tile_used.done(l, 8 * i + 4 * k + 3))
                        act.activation(adarow[:, ds(2 * P * i + P * k, P)], bank[6 + k][:, 0:P], ACT.Copy
                                       ).then_inc(ada_row.sem, 1)
                with act.Fori(0, FEAT_T // 4) as i:
                    for k in range(4):
                        act.wait_ge(tile_used.sem, tile_used.done(l, FEAT_AT + 4 * i + k))
                        act.activation(zT[:, ds(4 * i + k, 1), :].rearrange("p o t -> p (o t)"), bank[6 + k % 2][:, 0:T],
                                       ACT.Copy, scale=zscale[:, ds(4 * i + k, 1)]).then_inc(z_set.sem, 1)
                act.wait_ge(z_ps.sem, z_ps.done(l, 0))
                act.activation(zT[:, KI, :], bank[6][:, 0:T], ACT.Copy).then_inc(z_set.sem, 1)
                act.wait_ge(z_ps.sem, z_ps.done(l, 1))
                act.activation(zT[0:HI, WI, :], bank[7][0:HI, 0:T], ACT.Copy, scale=float(HI) ** -0.5
                               ).then_inc(z_set.sem, 1)
                for n in range(2 * HI):
                    w = P if n < HI else TP
                    act.wait_ge(pd_ps.sem, pd_ps.done(l, n))
                    act.wait_ge(pd_acc.sem, pd_acc.free(l, n))
                    act.activation(S[:, n % 2, 0:w], bank[1 + n % 2][:, 0:w], ACT.Relu).then_inc(pd_relu.sem, 1)
                act.wait_ge(pd_acc.sem, pd_acc.done(l, 2 * HI - 1))
                with act.Fori(0, NB // 2) as i:
                    for s in range(2):
                        act.wait_ge(sd_ps.sem, sd_ps.done(l, 2 * i + s))
                        act.wait_ge(sc_ps.sem, sc_ps.free(l, 2 * i + s))
                        act.activation(S[0:64, s, 0:PAST], psf[0:64, 1024 * s:1024 * s + PAST], ACT.Relu)
                        act.activation(S[0:64, s, PAST:L], bank[4][64 * s:64 * s + 64, 0:NT], ACT.Relu
                                       ).then_inc(sd_relu.sem, 1)

                def exp_unit(u):
                    act.wait_ge(u_logit.sem, u_logit.done(l, u.n))
                    v = S[0:u.rows, u.s, :]
                    act.activation(v, v, ACT.Exp, bias=nmx[0:u.rows, u.s, 0:1], accum_out=sm[0:u.rows, u.s, 0:1]
                                   ).then_inc(u_exp.sem, 1)

                with act.Fori(0, NB // 2) as i:
                    for r in range(4):
                        exp_unit(unit_ac(i, r))
                with act.Fori(0, NB // 2) as i:
                    for r in range(2):
                        exp_unit(unit_b(i, r))

                def exp_item(n):
                    qt, g, w, maps = item(n)
                    act.wait_ge(i_logit.sem, i_logit.done(l, n))
                    for m in range(maps):
                        v = S[:, n % 2, w * m:w * m + w]
                        ins = act.activation(v, v, ACT.Exp, bias=nmx[:, n % 2, m:m + 1],
                                             accum_out=sm[:, n % 2, m:m + 1])
                    ins.then_inc(i_exp.sem, 1)

                exp_item(0)
                for n in range(ITEMS):
                    qt, g, w, maps = item(n)
                    act.wait_ge(i_tp.sem, i_tp.done(l, n))
                    act.wait_ge(i_o.sem, i_o.free(l, n))
                    act.activation(PTf[:, n % 2, 0:2 * w], bank[4 + n % 2][:, 0:2 * w], ACT.Copy
                                   ).then_inc(i_tset.sem, 1)
                    e = n - ADA_FROM
                    if 0 < e < ADA_ITEMS and e % 2:
                        act.wait_ge(tile_used.sem, tile_used.done(l, ADA2_AT + 2 * e + 1))
                        act.activation(adarow[:, P * (e // 2):P * (e // 2) + P], bank[7][:, 0:P], ACT.Copy
                                       ).then_inc(ada_row2.sem, 1)
                    if n + 1 < ITEMS:
                        exp_item(n + 1)
                act.wait_ge(gn_ps.sem, gn_ps.done(l, 0))
                for c in range(2):
                    ins = act.activation(sq[:, c, :], bank[c][:, 0:T], ACT.Sqrt, bias=epsc[:])
                ins.then_inc(gn_std.sem, 1)

                def norm(j):
                    for k in range(KD):
                        act.wait_ge(ln_xc.sem, ln_xc.done(l, KD * j + k))
                        act.wait_ge(ln_mm.sem, ln_mm.free(l, KD * j + k))
                        act.activation(sq[:, k % 2, :], xT[:, k, :], ACT.Square).then_inc(ln_sq.sem, 1)
                    act.wait_ge(ln_mm.sem, ln_mm.done(l, KD * j + KD - 1))
                    act.activation(rstd[:], bank[1][:, 0:T], ACT.Sqrt, bias=epsc[:]).then_inc(ln_std.sem, 1)
                    for k in range(KD):
                        act.wait_ge(ln_n.sem, ln_n.done(l, KD * j + k))
                        g = P_LN + 2 * KD * j + k
                        act.activation(xT[:, k, :], xT[:, k, :], ACT.Identity, scale=par[:, g:g + 1],
                                       bias=par[:, g + KD:g + KD + 1]).then_inc(ln_x.sem, 1)

                norm(0)
                with act.Fori(0, UP_T // 4) as i:
                    for k in range(4):
                        act.wait_ge(tile_used.sem, tile_used.done(l, UP_AT + 4 * i + k))
                        act.wait_ge(up_set.sem, up_set.free(l, 4 * i + k))
                        act.activation(sq[:, k % 2, :], bank[6 + k % 2][:, 0:T], ACT.Relu).then_inc(up_relu.sem, 1)
                norm(1)

        @block.tensor
        def _(pe):
            for signal in (tile_used, u_s, u_tp, u_o, i_tp, i_o, ln_mm, sc_ps):
                pe.sem_inc(signal.sem, signal.spare)
            pe.wait_ge(ld_const, N_CONST)
            for c, (u0, u1) in enumerate(((0, 512), (512, 1024), (1024, NDIST))):
                pe.matmul(bank[c][0:H, 0:u1 - u0], relb[:], big[0:34, u0:u1], start=True, stop=True).then_inc(dist_ps, 1)
            pe.wait_ge(silu_done, 1)
            pe.wait_ge(zeroed, 1)

            def cached_wait(l, u, ld_ab, ld_c):
                if u.kind == "A":
                    pe.wait_ge(ld_ab, AB_LOADS * l + 16 * u.nth + 16)
                elif u.kind == "B":
                    pe.wait_ge(ld_ab, AB_LOADS * l + PAGES * u.nth + (A_LOADS + PAGES))
                else:
                    pe.wait_ge(ld_c, NB * PAGES * l + PAGES * u.b + PAGES)

            def logits(l, u):
                pe.wait_ge(q_set.sem, q_set.done(l, u.n))
                pe.wait_ge(u_logit.sem, u_logit.free(l, u.n))
                if not (isinstance(u.n, int) and u.n < 3):
                    pe.wait_ge(u_out.sem, u_out.done(l, u.n - 3))
                kv = cs[:, 0] if u.kind == "C" else ab[:, u.v, 0]
                cached_wait(l, u, ld_abk[u.v], ld_ck)
                lhs = qc[:, :] if u.kind == "C" else qab[:, 0 if u.kind == "A" else u.s, :]
                for q in range(3):
                    w = 512 if q < 2 else NT
                    at = 1536 * u.s + 512 * q
                    for c in range(u.chunks):
                        rhs = kv[:, 4 * q:4 * q + 4, P * c:P * c + P] if q < 2 else knew[:, u.s, c, :]
                        ins = pe.matmul(psf[G * c:G * c + G, at:at + w], lhs[:, G * c:G * c + G], rhs,
                                        start=True, stop=u.kind != "B")
                    if u.kind == "B":
                        for c in range(u.chunks):
                            ins = pe.matmul(psf[G * c:G * c + G, at:at + w], selcur[:, u.s, :],
                                            sel[:, 512 * q:512 * q + w], start=False, stop=True)
                pe.drain()
                pe.sem_inc(u_s.sem, 1)

            def turn(l, u):
                pe.wait_ge(u_exp.sem, u_exp.done(l, u.n))
                pe.wait_ge(u_tset.sem, u_tset.free(l, u.n))
                pe.sem_inc(passed, 1)
                r = u.rows
                for j in range(NPG + 1):
                    w, at = (P if j < NPG else NT), turned_at(u, j)
                    ins = pe.transpose(psf[0:w, at:at + r], S[0:r, u.s, P * j:P * j + w], ident[0:r, 0:r])
                ins.then_inc(u_tp.sem, 1)

            def values(l, u):
                pe.wait_ge(u_tset.sem, u_tset.done(l, u.n))
                pe.wait_ge(u_oset.sem, u_oset.free(l, u.n))
                cached_wait(l, u, ld_abv[u.v], ld_cv)
                pe.wait_ge(ld_vnew[u.v], 2 * 64 * l + (64 if u.kind == "B" else 0) + 16 * u.nth + 16)
                h = u.held
                for j in range(NPG + 1):
                    for c in range(u.chunks):
                        if j == NPG:
                            lhs, v0 = PT[0:NT, u.s, j, h * c:h * c + h], u.v0 + P * c
                            rhs = vnew[:, u.v, v0:v0 + P]
                        else:
                            lhs = PT[:, u.s, j, h * c:h * c + h]
                            rhs = (cs[:, 1] if u.kind == "C" else ab[:, u.v, 1])[:, j, P * c:P * c + P]
                        pe.matmul(bank[7][G * c:G * c + h, 0:P], lhs, rhs, start=j == 0, stop=j == NPG)
                pe.drain()
                pe.sem_inc(u_o.sem, 1)

            def turn_out(l, u):
                pe.wait_ge(u_oset.sem, u_oset.done(l, u.n))
                pe.wait_ge(u_out.sem, u_out.free(l, u.n))
                pe.sem_inc(passed, 1)
                c0 = outputs_at(u)
                if u.kind == "C":
                    ins = pe.matmul(psf[:, c0:c0 + G], osb[0:RC, u.s, :], sumC[:], start=True, stop=True)
                else:
                    ins = pe.transpose(psf[:, c0:c0 + RA], osb[:, u.s, :], ident[0:RA, 0:RA])
                ins.then_inc(u_ot.sem, 1)

            def step(l, unit, i, r, prev=True, following=True):
                turn(l, unit(i, r))
                if following:
                    logits(l, unit(i, r + 1))
                pe.wait_ge(u_tset.sem, u_tset.done(l, unit(i, r).n))
                if prev:
                    turn_out(l, unit(i, r - 1))
                values(l, unit(i, r))

            def ring_wait(l, s, at, i=0):
                pe.wait_ge(ld_w[s], l * (16 * TILES // RING) + 16 * (at // RING) + 16 * i + 16)

            def wide(s, kk):
                return ring[:, s].rearrange("p (e b) m -> p e (b m)", e=2)[:, kk, :]

            def h_wait(l, j, k):
                pe.wait_ge(h_prompt.sem, h_prompt.done(l, KD * j + k))
                pe.wait_ge(h_sample.sem, h_sample.done(l, KD * j + k))

            def chunks(l, at, n, rhs, freed, first=0):
                pe.sem_inc(passed, 1)
                with pe.Fori(first, n // RING) as i:
                    for s in range(RING):
                        pe.wait_ge(freed.sem, freed.free(l, RING * i + s))
                        ring_wait(l, s, at, i)
                        for k in range(KD):
                            ins = pe.matmul(bank[6 + s % 2][:, 0:T], ring[:, s, k, :], rhs[:, k, :],
                                            start=k == 0, stop=k == KD - 1)
                        ins.then_inc(tile_used.sem, 1)

            def norm_sums(l, j, summed):
                for k in range(KD):
                    pe.wait_ge(summed.sem, summed.done(l, k))
                    ins = pe.matmul(bank[0][:, 0:T], onesd[:], xT[:, k, :], start=k == 0, stop=k == KD - 1)
                ins.then_inc(ln_mean.sem, 1)
                for k in range(KD):
                    pe.wait_ge(ln_sq.sem, ln_sq.done(l, KD * j + k))
                    pe.matmul(bank[1][:, 0:T], onesd[:], sq[:, k % 2, :], start=k == 0, stop=k == KD - 1
                              ).then_inc(ln_mm.sem, 1)

            def ada_tile(ps, s):
                for kk in range(2):
                    for g in range(4):
                        pe.matmul(ps[G * g:G * g + G, 0:P], cz[:, 2 * s + kk, :], wide(s, kk)[:, P * g:P * g + P],
                                  start=s + kk == 0, stop=s == RING - 1 and kk == 1)
                pe.drain()
                pe.sem_inc(tile_used.sem, 1)

            def turn_ada():
                pe.sem_inc(passed, 1)
                for i in range(6):
                    ins = pe.transpose(psf[:, 1024 + P * i:1024 + P * i + P], adarow[:, P * i:P * i + P], ident[:])
                ins.then_inc(ada_tp.sem, 1)

            with pe.Fori(0, DEPTH) as l:
                pe.wait_ge(dn_set.sem, dn_set.free(l, 1))
                pe.sem_inc(passed, 1)
                with pe.Fori(0, 3) as i:
                    for k in range(2):
                        pe.wait_ge(ada_row.sem, ada_row.free(l, 2 * i + k))
                        for s in range(RING):
                            ring_wait(l, s, RING * k, 2 * i)
                            ada_tile(bank[6 + k], s)
                pe.wait_ge(ada_row.sem, ada_row.done(l, 5))
                turn_ada()
                for g in range(2):
                    for s in range(RING):
                        ring_wait(l, s, V_AT + RING * g)
                        for kk in range(2):
                            if g == 0:
                                h_wait(l, 0, 2 * s + kk)
                            for tt in range(3):
                                m = P if tt < 2 else TS
                                ins = pe.matmul(bank[3 * g + tt][0:m, :], hT[:, 2 * s + kk, P * tt:P * tt + m],
                                                wide(s, kk), start=s + kk == 0, stop=s == RING - 1 and kk == 1)
                        ins.then_inc(tile_used.sem, 1)
                chunks(l, FEAT_AT, FEAT_T, hT, z_set)
                pe.wait_ge(ld_wki, 16 * l + 16)
                for c, m in ((KI, P), (WI, HI)):
                    pe.wait_ge(z_set.sem, z_set.free(l, c))
                    for k in range(KD):
                        ins = pe.matmul(bank[6 + c % 2][0:m, 0:T], wki[:, k, P * (c - KI):P * (c - KI) + m], hT[:, k, :],
                                        start=k == 0, stop=k == KD - 1)
                    ins.then_inc(z_ps.sem, 1)
                pe.wait_ge(z_set.sem, z_set.done(l, WI))
                pe.wait_ge(v_set.sem, v_set.done(l, 5))
                pe.sem_inc(passed, 1)
                for qt in range(2):
                    pe.transpose(bank[0][:, HI * qt:HI * qt + HI], zT[0:HI, WI, P * qt:P * qt + P], ident[0:HI, 0:HI])
                pe.matmul(bank[0][0:64, 64:128], rep[:], zT[0:HI, WI, TP:T], start=True, stop=True
                          ).then_inc(wi_ps.sem, 1)
                for n in range(2 * HI):
                    qt, h = n // HI, n % HI
                    w = P if qt == 0 else TP
                    q = slice(64 * (h % 2), 64 * (h % 2) + 64)
                    pe.wait_ge(pd_relu.sem, pd_relu.free(l, n))
                    pe.matmul(bank[1 + n % 2][:, 0:w], zT[q, QI + h // 2, P * qt:P * qt + P], zT[q, KI, 0:w],
                              start=True, stop=True).then_inc(pd_ps.sem, 1)
                pe.wait_ge(pd_relu.sem, pd_relu.done(l, 2 * HI - 1))
                pe.wait_ge(wi_set.sem, wi_set.done(l, 0))
                spans = ((0, 512), (1, 512), (2, NT))
                for q, w in spans:
                    pe.matmul(bank[5 + q][0:TS, 0:w], zero16[:, 0:TS], zero16[:, 0:w], start=True, stop=False)
                for i in range(NB // 2):
                    for s in range(2):
                        b = 2 * i + s
                        pe.wait_ge(qi_set.sem, qi_set.done(l, b))
                        pe.wait_ge(ld_ik[b % IK_SLOTS], NB // IK_SLOTS * PAGES * l + PAGES * (b // IK_SLOTS + 1))
                        pe.wait_ge(sd_relu.sem, sd_relu.free(l, 2 * i + s))
                        for q in range(2):
                            pe.matmul(bank[2 * s + q][0:64, :], qi[:, s, :],
                                      ik[:, b % IK_SLOTS, 4 * q:4 * q + 4, :],
                                      start=True, stop=True)
                        pe.matmul(bank[4][64 * s:64 * s + 64, 0:NT], qi[:, s, :],
                                  kin[:, s, :], start=True, stop=True).then_inc(sd_ps.sem, 1)
                    for s in range(2):
                        pe.wait_ge(sd_relu.sem, sd_relu.done(l, 2 * i + s))
                        pe.sem_inc(passed, 1)
                        for q, w in spans:
                            ins = pe.matmul(bank[5 + q][0:TS, 0:w], wcur[:, s, :], S[0:64, s, 512 * q:512 * q + w],
                                            start=False, stop=False)
                        ins.then_inc(sc_ps.sem, 1)
                for q, w in spans:
                    ins = pe.matmul(bank[5 + q][0:TS, 0:w], zero16[:, 0:TS], zero16[:, 0:w], start=False, stop=True)
                ins.then_inc(sc_sum.sem, 1)
                pe.wait_ge(sc_copied.sem, sc_copied.done(l, 0))
                logits(l, unit_ac(0, 0))
                step(l, unit_ac, 0, 0, prev=False)
                with pe.Fori(0, 3) as i:
                    for r in range(1, 5):
                        step(l, unit_ac, i, r)
                for r in range(1, 4):
                    step(l, unit_ac, 3, r, following=r < 3)
                turn_out(l, unit_ac(3, 3))
                pe.wait_ge(sel_set.sem, sel_set.done(l, 0))
                pe.wait_ge(u_out.sem, u_out.done(l, AC_UNITS - 1))
                logits(l, unit_b(0, 0))
                step(l, unit_b, 0, 0, prev=False)
                with pe.Fori(0, 3) as i:
                    for r in range(1, 3):
                        step(l, unit_b, i, r)
                step(l, unit_b, 3, 1, following=False)
                turn_out(l, unit_b(3, 1))

                def item_logits(n):
                    qt, g, w, maps = item(n)
                    s = n % 2
                    pe.wait_ge(i_logit.sem, i_logit.free(l, n))
                    for m in range(maps):
                        if m == 2:
                            pe.drain()
                        at = 1024 * s + 512 * (m % 2) + w * (m // 2)
                        dst = psf[:, at:at + w]
                        if g < 6:
                            q, cq, ck = slice(64 * m, 64 * m + 64), QA + g, KA + g
                        else:
                            q, cq, ck = slice(32 * m, 32 * m + 32), QC + g - 6, KC + g - 6
                        topk = 3 <= g < 6
                        ins = pe.matmul(dst, zT[q, cq, P * qt:P * qt + P], zT[q, ck, 0:w], start=True, stop=not topk)
                        if topk:
                            ins = pe.matmul(dst, ident16[:], psel[:, psel_at[qt]:psel_at[qt] + w], start=False, stop=True)
                    ins.then_inc(i_s.sem, 1)

                def item_outputs(n):
                    qt, g, w, maps = item(n)
                    s = n % 2
                    pe.wait_ge(i_tset.sem, i_tset.done(l, n))
                    pe.wait_ge(i_out.sem, i_out.free(l, n))
                    for kt in range(w // P):
                        ins = pe.matmul(bank[6][:, 2 * P * s:2 * P * s + 2 * P], vp[:, kt, P * g:P * g + P],
                                        PTf[:, s, 2 * P * kt:2 * P * kt + 2 * P], start=kt == 0, stop=kt == w // P - 1)
                    ins.then_inc(i_o.sem, 1)

                pe.wait_ge(u_out.sem, u_out.done(l, UNITS - 1))
                pe.wait_ge(psel_set.sem, psel_set.done(l, 0))
                item_logits(0)
                for n in range(ITEMS):
                    if n + 1 < ITEMS:
                        item_logits(n + 1)
                    e = n - ADA_FROM
                    if 0 <= e < ADA_ITEMS:
                        if e % 2 == 0:
                            pe.wait_ge(ada_row2.sem, ada_row2.free(l, e // 2))
                        for k in (2 * e % RING, 2 * e % RING + 1):
                            ring_wait(l, k, ADA2_AT + 2 * e // RING * RING)
                            ada_tile(bank[7], k)
                    qt, g, w, maps = item(n)
                    s = n % 2
                    pe.wait_ge(i_p.sem, i_p.done(l, n))
                    pe.wait_ge(i_tset.sem, i_tset.free(l, n))
                    for kt in range(w // P):
                        for e in range(2):
                            m0 = w * (e if g < 6 else 2 * e) + P * kt
                            ins = pe.transpose(bank[4 + s][:, 2 * P * kt + P * e:2 * P * kt + P * e + P],
                                               S[:, s, m0:m0 + P], ident[:])
                    ins.then_inc(i_tp.sem, 1)
                    if n:
                        item_outputs(n - 1)
                item_outputs(ITEMS - 1)
                pe.wait_ge(ada_row2.sem, ada_row2.done(l, 5))
                turn_ada()
                pe.wait_ge(gn_sq.sem, gn_sq.done(l, 0))
                for c in range(2):
                    ins = pe.matmul(bank[c][:, 0:T], oneshd[:], sq[:, c, :], start=True, stop=True)
                ins.then_inc(gn_ps.sem, 1)
                pe.wait_ge(gn_set.sem, gn_set.done(l, 0))
                chunks(l, WO_AT, WO_T, oT, wo_set)
                norm_sums(l, 0, wo_set)
                pe.wait_ge(up_relu.sem, up_relu.free(l, 0))
                ring_wait(l, 0, UP_AT)
                for k in range(KD):
                    h_wait(l, 1, k)
                    ins = pe.matmul(bank[6][:, 0:T], ring[:, 0, k, :], hT[:, k, :], start=k == 0, stop=k == KD - 1)
                ins.then_inc(tile_used.sem, 1)
                for m in range(1, RING):
                    pe.wait_ge(up_relu.sem, up_relu.free(l, m))
                    ring_wait(l, m, UP_AT)
                    for k in range(KD):
                        ins = pe.matmul(bank[6 + m % 2][:, 0:T], ring[:, m, k, :], hT[:, k, :],
                                        start=k == 0, stop=k == KD - 1)
                    ins.then_inc(tile_used.sem, 1)
                chunks(l, UP_AT, UP_T, hT, up_relu, 1)
                pe.wait_ge(up_set.sem, up_set.done(l, FF // P - 1))
                pe.sem_inc(passed, 1)
                with pe.Fori(0, KD // 2) as i:
                    for m in range(2):
                        pe.wait_ge(dn_set.sem, dn_set.free(l, 2 * i + m))
                        for s in range(RING):
                            ring_wait(l, s, DOWN_AT + RING * m, 2 * i)
                            for k in range(KD):
                                ins = pe.matmul(bank[6 + m][:, 0:T], ring[:, s, k, :], uT[:, KD * s + k, :],
                                                start=s + k == 0, stop=s == RING - 1 and k == KD - 1)
                            ins.then_inc(tile_used.sem, 1)
                norm_sums(l, 1, dn_set)

        @block.vector
        def _(dve):
            for signal in (pd_acc, u_logit, u_tset, u_oset, u_out, i_logit, i_out, wo_set, dn_set, up_set):
                dve.sem_inc(signal.sem, signal.spare)
            dve.wait_ge(ld_const, N_CONST)
            dve.tensor_tensor(lp.rearrange("p (l e) d -> p l e d", e=2), lamb[:, :, 0::2, :], lamb[:, :, 1::2, :],
                              ALU.mult)
            dve.drain()
            dve.tensor_reduce(ls[:], lp, AX_X, ALU.add).then_inc(lam_sum, 1)
            for c, (u0, u1) in enumerate(((0, 512), (512, 1024), (1024, NDIST))):
                dve.wait_ge(dist_ps, c + 1)
                dve.tensor_copy(distb[:, u0:u1], bank[c][0:H, 0:u1 - u0]).then_inc(dist_sb, 1)
            dve.wait_ge(sig_exp, 1)
            dve.tensor_scalar(sgm[:], sgm[:], 1.0, None, ALU.add)
            dve.drain()
            dve.reciprocal(sgm[:], sgm[:])
            dve.drain()
            dve.wait_ge(zeroed, 1)
            dve.tensor_tensor(cz[:, :, 0:NCOND], cT[:], sgm[:], ALU.mult).then_inc(silu_done, 1)
            dve.wait_ge(lam_exp, 1)
            for l in range(DEPTH):
                nlam = par_all[:, l, P_NLAM:P_NLAM + 1]
                dve.tensor_tensor(nlam, ls[:, 2 * l + 1:2 * l + 2], ls[:, 2 * l:2 * l + 1], ALU.subtract)
                dve.drain()
                dve.tensor_scalar(nlam, nlam, -LAM_INIT[l], None, ALU.add)
                sub = par_all[:, l, P_SUB:P_SUB + 1]
                dve.tensor_scalar(sub, sub, 1.0 - LAM_INIT[l], None, ALU.mult)
                dve.drain()
                dve.scalar_tensor_tensor(par_all[:, l, P_COEF:P_COEF + 1], nlam, ismap1[:, 0:1], ismap1[:, 1:2],
                                         ALU.mult, ALU.add)
            dve.drain()

            def modulation(l, j):
                dve.wait_ge(ada_tp.sem, ada_tp.done(l, j))
                b0 = P_ADA + 24 * j
                dve.tensor_tensor(adaT[:, j], psf[:, 1024:1024 + 24 * G].rearrange("p (c n) -> p c n", n=G)[:, :, 0:NCOND],
                                  repeat(par[:, b0:b0 + 24], NCOND), ALU.add)
                dve.drain()
                dve.tensor_scalar(adaT[:, j, KD:24, :], adaT[:, j, KD:24, :], 1.0, None, ALU.add
                                  ).then_inc(ada_set.sem, 1)
                dve.drain()

            def modulate(j, k):
                dve.tensor_scalar(hT[:, k, 0:TP], xT[:, k, 0:TP], adaT[:, j, KD + k, 0:1], adaT[:, j, k, 0:1],
                                  ALU.mult, ALU.add).then_inc(h_prompt.sem, 1)

            def residual(j, m, ps, slot, signal):
                t = sq[:, slot, :]
                g = adaT[:, j, ds(2 * KD + m, 1), :].rearrange("p o n -> p (o n)")
                dve.tensor_scalar(t[:, 0:TP], ps[:, 0:TP], g[:, 0:1], None, ALU.mult)
                dve.tensor_tensor(t[:, TP:T].rearrange("p (b t) -> p b t", t=NT),
                                  ps[:, TP:T].rearrange("p (b t) -> p b t", t=NT), repeat(g[:, 1:NCOND], NT), ALU.mult)
                dve.drain()
                x = xT[:, ds(m, 1), :].rearrange("p o t -> p (o t)")
                dve.scalar_tensor_tensor(x, x, ALPHA, t, ALU.mult, ALU.add).then_inc(signal.sem, 1)

            def norm(l, j):
                dve.wait_ge(ln_mean.sem, ln_mean.done(l, j))
                for k in range(KD):
                    dve.tensor_tensor(xT[:, k, :], xT[:, k, :], bank[0][:, 0:T], ALU.subtract).then_inc(ln_xc.sem, 1)
                dve.wait_ge(ln_std.sem, ln_std.done(l, j))
                dve.reciprocal(rstd[:], rstd[:])
                dve.drain()
                for k in range(KD + 2):
                    if k < KD:
                        dve.tensor_tensor(xT[:, k, :], xT[:, k, :], rstd[:], ALU.mult).then_inc(ln_n.sem, 1)
                    if j == 0 and k >= 2:
                        dve.wait_ge(ln_x.sem, ln_x.done(l, k - 2))
                        modulate(1, k - 2)

            def read_logits(l, u):
                dve.wait_ge(u_s.sem, u_s.done(l, u.n))
                dve.wait_ge(u_tp.sem, u_tp.free(l, u.n))
                dve.sem_inc(passed, 1)
                r = u.rows
                bias = {"A": sbiasA, "B": sbiasB, "C": sbiasC}[u.kind]
                dve.tensor_tensor_reduce(out=S[0:r, u.s, :], in0=psf[0:r, 1536 * u.s:1536 * u.s + L], in1=bias[:],
                                         scale=1.0, scalar=-3e38, op0=ALU.add, op1=ALU.max,
                                         accum_out=mx[0:r, u.s, 0:1])
                dve.drain()
                dve.tensor_scalar(nmx[0:r, u.s, 0:1], mx[0:r, u.s, 0:1], -1.0, None, ALU.mult).then_inc(u_logit.sem, 1)

            def read_turned(l, u):
                dve.wait_ge(u_tp.sem, u_tp.done(l, u.n))
                dve.wait_ge(u_o.sem, u_o.free(l, u.n))
                h, n = u.held, min(NPG, 512 // u.rows)
                for j0, j1 in ((0, n), (n, NPG), (NPG, NPG + 1)):
                    if j0 < j1:
                        p1 = P if j1 <= NPG else NT
                        first = psf[0:p1, turned_at(u, j0):turned_at(u, j0) + h]
                        to = PT[0:p1, u.s, j0, 0:h]
                        ins = dve.tensor_copy(
                            bass.AP(to.tensor, to.offset, [list(to.ap[0]), [64, j1 - j0], [h, u.chunks], [1, h]]),
                            bass.AP(first.tensor, first.offset,
                                    [list(first.ap[0]), [u.rows, j1 - j0], [G, u.chunks], [1, h]]))
                ins.then_inc(u_tset.sem, 1)

            def read_outputs(l, u):
                r = u.rows
                dve.wait_ge(u_o.sem, u_o.done(l, u.n))
                dve.reciprocal(rs[0:r, u.s, 0:1], sm[0:r, u.s, 0:1])
                dve.drain()
                src, dst = bank[7][0:r, 0:P], osb[0:r, u.s, :]
                if u.kind == "C":
                    ins = dve.tensor_scalar(dst, src, rs[0:r, u.s, 0:1], par[0:r, P_COEF:P_COEF + 1], ALU.mult, ALU.mult)
                else:
                    ins = dve.tensor_scalar(dst, src, rs[0:r, u.s, 0:1], None, ALU.mult)
                ins.then_inc(u_oset.sem, 1)

            def place_outputs(l, u):
                dve.wait_ge(u_ot.sem, u_ot.done(l, u.n))
                c0 = outputs_at(u)
                n, gap, m0 = (2, 2 * NT, 6) if u.kind == "C" else (3, G, 0 if u.kind == "A" else 3)
                for half in range(2):
                    q = slice(64 * half, 64 * half + 64)
                    first = psf[q, c0 + NT * half:c0 + NT * half + NT]
                    ins = dve.tensor_copy(oT[q, m0:m0 + n, ds(TP + NT * u.b, NT)],
                                          bass.AP(first.tensor, first.offset, [list(first.ap[0]), [gap, n], [1, NT]]))
                ins.then_inc(u_out.sem, 1)

            def take8():
                dve.max(m8[0:TS, 0, :], work[:])
                dve.drain()
                dve.match_replace(work[:], m8[0:TS, 0, :], work[:], TAKEN)
                dve.drain()

            def step(l, unit, i, r, prev=True, following=True, select=False):
                if prev:
                    read_outputs(l, unit(i, r - 1))
                read_turned(l, unit(i, r))
                if select:
                    take8()
                if following:
                    read_logits(l, unit(i, r + 1))
                if prev:
                    place_outputs(l, unit(i, r - 1))
                if select:
                    take8()

            with dve.Fori(0, DEPTH) as l:
                dve.wait_ge(ln_x.sem, ln_x.free(l, 0))
                dve.tensor_copy(par[:], par_all[:, ds(l, 1), :].rearrange("p o n -> p (o n)"))
                dve.drain()
                modulation(l, 0)
                for k in range(KD):
                    modulate(0, k)
                for g in range(2):
                    dve.wait_ge(tile_used.sem, tile_used.done(l, V_AT + 4 * g + 3))
                    for tt in range(3):
                        dst = vp[:, tt, 512 * g:512 * g + 512] if tt < 2 else vs[:, 512 * g:512 * g + 512]
                        dve.tensor_copy(dst, bank[3 * g + tt][0:P if tt < 2 else TS, :]).then_inc(v_set.sem, 1)
                dve.wait_ge(wi_ps.sem, wi_ps.done(l, 0))
                dve.tensor_copy(wiq[:].rearrange("p a b -> p (a b)"), bank[0][:, 0:2 * HI])
                first = wall[:, 0, 0:NT]
                dve.tensor_tensor(bass.AP(first.tensor, first.offset, [list(first.ap[0]), [TS + NT, NB], [1, NT]]),
                                  bank[0][0:64, 64:128].rearrange("p (b t) -> p b t", t=NT),
                                  tmask[:].rearrange("p (b t) -> p b t", t=NT), ALU.mult).then_inc(wi_set.sem, 1)
                dve.drain()
                for n in range(2 * HI):
                    qt, h = n // HI, n % HI
                    w, at = (P, psel_at[0]) if qt == 0 else (TP, psel_at[1])
                    dve.wait_ge(pd_relu.sem, pd_relu.done(l, n))
                    dve.scalar_tensor_tensor(psc[:, at:at + w], S[:, n % 2, 0:w], wiq[:, qt, h:h + 1],
                                             cmask[:, TP - w:TP] if h == 0 else psc[:, at:at + w], ALU.mult, ALU.add
                                             ).then_inc(pd_acc.sem, 1)
                    dve.drain()
                blocks = [(psel_at[0], P), (psel_at[1], TP)]
                for _ in range(TOPK_P // 8):
                    for e, (at, w) in enumerate(blocks):
                        dve.max(m8[:, e, :], psc[:, at:at + w])
                    dve.drain()
                    for e, (at, w) in enumerate(blocks):
                        dve.match_replace(psc[:, at:at + w], m8[:, e, :], psc[:, at:at + w], TAKEN)
                    dve.drain()
                dve.tensor_scalar(psel[:], psc[:], TAKEN / 2, FAR, ALU.is_gt, ALU.mult).then_inc(psel_set.sem, 1)
                dve.wait_ge(sc_sum.sem, sc_sum.done(l, 0))
                dve.tensor_copy(work[:, 0:PAST], psf[0:TS, 5 * 512:5 * 512 + PAST])
                dve.tensor_tensor(work[:, PAST:L], bank[7][0:TS, 0:NT], smask[:], ALU.add).then_inc(sc_copied.sem, 1)
                dve.drain()
                dve.wait_ge(ld_dist, N_DIST)
                read_logits(l, unit_ac(0, 0))
                step(l, unit_ac, 0, 0, prev=False, select=True)
                with dve.Fori(0, 3) as i:
                    for r in range(1, 5):
                        step(l, unit_ac, i, r, select=True)
                for r in range(1, 4):
                    step(l, unit_ac, 3, r, following=r < 3, select=True)
                dve.tensor_scalar(sel[0:TS, :], work[:], TAKEN / 2, FAR, ALU.is_gt, ALU.mult).then_inc(sel_set.sem, 1)
                read_outputs(l, unit_ac(3, 3))
                place_outputs(l, unit_ac(3, 3))
                read_logits(l, unit_b(0, 0))
                step(l, unit_b, 0, 0, prev=False)
                with dve.Fori(0, 3) as i:
                    for r in range(1, 3):
                        step(l, unit_b, i, r)
                step(l, unit_b, 3, 1, following=False)
                read_outputs(l, unit_b(3, 1))
                place_outputs(l, unit_b(3, 1))

                def item_read(n):
                    qt, g, w, maps = item(n)
                    s = n % 2
                    dve.wait_ge(i_s.sem, i_s.done(l, n))
                    dve.wait_ge(i_tp.sem, i_tp.free(l, n))
                    for e in range(maps // 2):
                        v = slice(2 * w * e, 2 * w * e + 2 * w)
                        first = psf[:, 1024 * s + w * e:1024 * s + w * e + w]
                        ps = bass.AP(first.tensor, first.offset, [list(first.ap[0]), [512, 2], [1, w]])
                        if g < 6:
                            bias = pbias[:, 2 * g:2 * g + 2, TP - w:TP]
                        else:
                            row = pbias[:, HA + HB + 2 * (g - 6) + e, TP - w:TP]
                            bias = bass.AP(row.tensor, row.offset, [list(row.ap[0]), [0, 2], [1, w]])
                        dve.tensor_tensor(S[:, s, v].rearrange("p (m w) -> p m w", w=w),
                                          ps, bias, ALU.add)
                    dve.drain()
                    dve.tensor_reduce(mx[:, s, 0:maps], S[:, s, 0:maps * w].rearrange("p (m w) -> p m w", w=w), AX_X,
                                      ALU.max)
                    dve.drain()
                    dve.tensor_scalar(nmx[:, s, 0:maps], mx[:, s, 0:maps], -1.0, None, ALU.mult
                                      ).then_inc(i_logit.sem, 1)

                def item_out(n):
                    qt, g, w, maps = item(n)
                    dve.wait_ge(i_o.sem, i_o.done(l, n))
                    for e in range(2):
                        q = slice(64 * e, 64 * e + 64)
                        ins = dve.tensor_copy(oT[q, g, P * qt:P * qt + P], bank[6][q, P * (2 * (n % 2) + e):P * (2 * (n % 2) + e) + P])
                    ins.then_inc(i_out.sem, 1)

                item_read(0)
                for n in range(ITEMS):
                    qt, g, w, maps = item(n)
                    s = n % 2
                    dve.wait_ge(i_exp.sem, i_exp.done(l, n))
                    dve.reciprocal(rs[:, s, 0:maps], sm[:, s, 0:maps])
                    dve.drain()
                    for e in range(2):
                        m = e if g < 6 else 2 * e
                        v = S[:, s, w * m:w * m + w]
                        ins = dve.tensor_scalar(v, v, rs[:, s, m:m + 1], None, ALU.mult)
                        if g >= 6:
                            dve.tensor_scalar(rs[:, s, m + 1:m + 2], rs[:, s, m + 1:m + 2], par[:, P_NLAM:P_NLAM + 1],
                                              None, ALU.mult)
                    if g >= 6:
                        dve.drain()
                        for m in (0, 2):
                            v, v2 = (S[:, s, w * k:w * k + w] for k in (m, m + 1))
                            ins = dve.scalar_tensor_tensor(v, v2, rs[:, s, m + 1:m + 2], v, ALU.mult, ALU.add)
                    ins.then_inc(i_p.sem, 1)
                    if n + 1 < ITEMS:
                        item_read(n + 1)
                    if n:
                        item_out(n - 1)
                item_out(ITEMS - 1)
                dve.drain()
                dve.tensor_tensor(sq[:], oT[:, 6:8, :], oT[:, 6:8, :], ALU.mult).then_inc(gn_sq.sem, 1)
                modulation(l, 1)
                dve.wait_ge(gn_std.sem, gn_std.done(l, 0))
                dve.reciprocal(sq[:], sq[:])
                dve.drain()
                dve.scalar_tensor_tensor(oT[:, 6:8, :], oT[:, 6:8, :], par[:, P_SUB:P_SUB + 1], sq[:], ALU.mult,
                                         ALU.mult).then_inc(gn_set.sem, 1)
                with dve.Fori(0, WO_T // 2) as i:
                    for m in range(2):
                        dve.wait_ge(tile_used.sem, tile_used.done(l, WO_AT + 2 * i + m))
                        residual(0, 2 * i + m, bank[6 + m], m, wo_set)
                norm(l, 0)
                with dve.Fori(0, UP_T // 2) as i:
                    for k in range(2):
                        dve.wait_ge(up_relu.sem, up_relu.done(l, 2 * i + k))
                        dve.tensor_tensor(uT[:, ds(2 * i + k, 1), :].rearrange("p o t -> p (o t)"), sq[:, k, :],
                                          sq[:, k, :], ALU.mult).then_inc(up_set.sem, 1)
                with dve.Fori(0, KD // 2) as i:
                    for m in range(2):
                        dve.wait_ge(tile_used.sem, tile_used.done(l, DOWN_AT + 8 * i + 4 * m + 3))
                        residual(1, 2 * i + m, bank[6 + m], m, dn_set)
                norm(l, 1)


def bucket(dist):
    exact, n_buckets, far = 16, 32, 128
    n = max(dist, 0)
    if n < exact:
        return n
    return min(exact + int(math.log(n / exact) / math.log(far / exact) * (n_buckets - exact)), n_buckets - 1)


def constants():
    dist = DIST0 - np.arange(NDIST)
    onehot = np.zeros((34, NDIST), np.float32)
    onehot[[bucket(d) for d in dist], np.arange(NDIST)] = 1
    held = np.zeros(NDIST)
    for win, dil in ((128, 1), (512, 4), (2048, 16)):
        held += (dist >= 0) & (dist <= win) & (dist % dil == 0)
    onehot[32] = np.where(held > 0, np.log(np.maximum(held, 1)), FAR)
    onehot[33] = np.where(dist >= 0, 0, FAR)
    relrows = np.zeros((2, H), np.float32)
    relrows[0, :HA] = 1
    relrows[1, HA:] = 1
    zscale = np.ones((P, NZ), np.float32)
    zscale[:, QI:QC] = DH ** -0.5
    zscale[:, QC:KA] = DC ** -0.5
    hd = np.arange(P) // DH
    ht = np.arange(HI * NT)
    bt = np.arange(TS)
    selB = np.zeros((TS, NB, G), np.float32)
    for b in range(NB):
        for r in range(2 * NT):
            selB[b * NT + r % NT, b, r] = 1
    sumC = np.zeros((RC, 32), np.float32)
    for r in range(RC):
        sumC[r, r // 16 * NT + r % NT] = 1
    is1 = ((np.arange(P) // NT) % 2 == 1).astype(np.float32)
    p, j = np.arange(P)[:, None], np.arange(TP)[None]
    t, u = np.arange(TS)[:, None] % NT, np.arange(NT)[None]
    f, bf = np.float32, mybir.dt.np(BF16)
    return {
        "ident": np.eye(P, dtype=f), "ident16": np.eye(P).astype(bf),
        "onesd": np.full((P, P), 1 / D, f), "oneshd": ((hd[:, None] == hd[None]) / DH).astype(f),
        "zscale": zscale, "relrows": relrows, "onehot": onehot,
        "rep": (np.arange(HI)[:, None] == ht[None] // NT).astype(f),
        "tmask": (ht[:, None] % NT == bt[None] % NT).astype(f),
        "selB": selB.astype(bf), "sumC": sumC, "ismap1": np.stack([is1, 1 - is1], 1),
        "cmask": np.where(P + p - j >= 0, 0, FAR).astype(f), "smask": np.where(t >= u, 0, FAR).astype(f),
    }


def kernel(**inputs):
    import concourse.bacc as bacc
    from concourse.bass_utils import run_bass_kernel_spmd

    v = {k: np.asarray(x) for k, x in inputs.items()}

    def narrow(w):
        return w.reshape(-1, KD, P, w.shape[1] // P, P).transpose(3, 0, 2, 1, 4).reshape(-1, P, KD * P)

    def wide(w):
        return w.reshape(4, 2, P, w.shape[1] // 512, 512).transpose(3, 0, 2, 1, 4).reshape(-1, P, KD * P)

    names = ("qa", "ka", "va", "qb", "kb", "vb", "qi", "ki", "wi", "qc", "kc", "vc")
    sizes = (384, 384, 384, 384, 384, 384, 512, 64, 8, 256, 256, 256)
    at = dict(zip(names, np.cumsum((0,) + sizes[:-1])))
    tiles, wki = [], []
    for l in range(DEPTH):
        part = {n: v["w_in"][l][:, at[n]:at[n] + s] for n, s in zip(names, sizes)}
        tiles += [wide(v["w_ada_mix"][l]),
                  wide(np.concatenate([part[n] for n in ("va", "vb", "vc")], 1)),
                  narrow(np.concatenate([part[n] for n in ("qi", "qa", "qb", "qc", "ka", "kb", "kc")], 1)),
                  wide(v["w_ada_mlp"][l]), narrow(v["w_o"][l]), narrow(v["w_up"][l]), narrow(v["w_down"][l])]
        w = np.concatenate([part["ki"], part["ki"], part["wi"]], 1)
        wki.append(w.reshape(KD, P, -1).transpose(1, 0, 2))

    def turned(k):
        n, _, f = k.shape
        return k.transpose(0, 2, 1).reshape(n, f // P, P, PAGE).transpose(0, 2, 1, 3).reshape(n, P, f)

    n_pool = DEPTH * N_PHYS
    ca = np.stack([turned(v["cache_a_k"].reshape(-1, P, 384)), v["cache_a_v"].reshape(-1, P, 384)])
    ki = v["cache_b_ik"].reshape(n_pool, P, DH).transpose(0, 2, 1)
    chunk = lambda x: x.reshape(x.shape[:-1] + (-1, P))
    cols = lambda x: np.moveaxis(chunk(x), -1, 0)
    params = np.concatenate([
        cols(v["b_ada_mix"]), cols(v["b_ada_mlp"]), cols(v["ln1_g"]), cols(v["ln1_b"]), cols(v["ln2_g"]),
        cols(v["ln2_b"]), np.tile(v["subln_g"], (1, 2)).T[:, :, None]], 2)
    xs = np.concatenate([v["x_prompt"].reshape(TP, D), v["x_sample"].reshape(TS, D)])
    cond = np.concatenate([v["c_prompt"], v["c_sample"]])
    arrays = {
        "x": xs.reshape(T, KD, P).transpose(2, 1, 0), "cond": cond.reshape(NCOND, KD, P).transpose(2, 1, 0),
        "rel_bias": v["rel_bias"], "lam": v["lam"].reshape(1, -1), "page_table": v["page_table"].reshape(1, -1),
        "params": params, "tiles": np.concatenate(tiles), "wki": np.stack(wki),
        "cache_a": ca.reshape(2, DEPTH * NB, NPG, P, -1).transpose(1, 3, 0, 2, 4).reshape(DEPTH * NB, P, -1),
        "pool_bk": turned(v["cache_b_k"].reshape(n_pool, P, 384)), "pool_bv": v["cache_b_v"].reshape(n_pool, P, 384),
        "pool_ck": turned(v["cache_c_k"].reshape(n_pool, P, 256)), "pool_cv": v["cache_c_v"].reshape(n_pool, P, 256),
        "pool_ik": np.concatenate([ki, ki], 1),
        **constants(),
    }
    shapes = {"y": (P, KD, T), "z": (DEPTH, P, KI + 1 - KA, T), "vp": (DEPTH, P, 2, D), "vs": (DEPTH, TS, D),
              "cache_a": (DEPTH * NB, P, 2 * A_W)}
    nc = bacc.Bacc("TRN2", target_bir_lowering=False, num_devices=1, dynamic_dma_scratch_size=1024)
    ins, feeds = {}, {}
    for name, x in arrays.items():
        x = np.ascontiguousarray(x)
        feeds[f"in_{name}"] = x
        ins[name] = nc.dram_tensor(f"in_{name}", x.shape, mybir.dt.from_np(x.dtype), kind="ExternalInput").ap()
    outs = {n: nc.dram_tensor(f"out_{n}", s, F32, kind="ExternalOutput").ap() for n, s in shapes.items()}
    program(nc, ins, outs)
    r = run_bass_kernel_spmd(nc, [feeds], core_ids=[0]).results[0]
    got = {n: np.asarray(r[f"out_{n}"]).reshape(s) for n, s in shapes.items()}

    y = got["y"].transpose(2, 1, 0).reshape(T, D)
    z = got["z"].transpose(0, 3, 2, 1).reshape(DEPTH, T, -1)
    ka, kb, kc, ki = z[..., 0:384], z[..., 384:768], z[..., 768:1024], z[..., 1024:1024 + DH]
    vpr = got["vp"].transpose(0, 2, 1, 3).reshape(DEPTH, TP, D)
    vsm = got["vs"]
    c = got["cache_a"].reshape(DEPTH, NB, P, 2, NPG, 384)
    c_k = c[:, :, :, 0].reshape(DEPTH, NB, P, NPG, 3, P).transpose(0, 1, 3, 5, 4, 2).reshape(DEPTH, NB, PAST, 384)
    c_v = c[:, :, :, 1].transpose(0, 1, 3, 2, 4).reshape(DEPTH, NB, PAST, 384)
    pr = lambda x, *s: np.ascontiguousarray(x).reshape(DEPTH, 1, TP, *s)
    sm = lambda x, *s: np.ascontiguousarray(x).reshape(DEPTH, NB, NT, *s)
    p, s = slice(0, TP), slice(TP, T)
    new_k = np.concatenate([c_k.reshape(DEPTH, NB, PAST, HA, DH), sm(ka[:, s], HA, DH)], 2)
    new_v = np.concatenate([c_v.reshape(DEPTH, NB, PAST, HA, DH), sm(vsm[..., VA:VB], HA, DH)], 2)
    return (y[p].reshape(1, TP, D).copy(), y[s].reshape(NB, NT, D).copy(),
            pr(ka[:, p], HA, DH), pr(vpr[..., VA:VB], HA, DH), pr(kb[:, p], HB, DH), pr(vpr[..., VB:VC], HB, DH),
            pr(ki[:, p], DH), pr(kc[:, p], HC, 2, DC), pr(vpr[..., VC:], HC, 2 * DC),
            new_k, new_v, sm(kb[:, s], HB, DH), sm(vsm[..., VB:VC], HB, DH), sm(ki[:, s], DH),
            sm(kc[:, s], HC, 2, DC), sm(vsm[..., VC:], HC, 2 * DC))
```
